# Optimizing a Trainium2 kernel written in Bass

```python
import functools
import jax, jax.numpy as jnp
from jax import lax
import numpy as np

D_MODEL = 1024
BATCH = 1
SEQ = 2048
DEPTH = 1
DEC_BATCH = 8
DEC_SEQ = 16
PAST_LEN = 1024

CHUNK = 64
HEAD_DIM = 64
N_HEADS_A = 8
N_HEADS_B = 8
WIDTH_A = N_HEADS_A * HEAD_DIM
WIDTH_B = N_HEADS_B * HEAD_DIM
MIX_WIDTH = WIDTH_A + WIDTH_B
Q_BLOCK = 128
LEFT_CHUNKS = 8
LEFT_REACH = LEFT_CHUNKS * CHUNK
BAND = LEFT_REACH + CHUNK
REL_CLIP = 128
D_FF = -(-(8 * D_MODEL) // (3 * 256)) * 256
D_IN = 3 * WIDTH_A + N_HEADS_A + 3 * WIDTH_B
EPS = 1e-6
SCALE = HEAD_DIM ** -0.5

kernel_name = "hymba_fox_chunkband_stream_encoder"

def rmsnorm(x, g):
    xf = x.astype(jnp.float32)
    y = xf * lax.rsqrt(jnp.mean(xf * xf, axis=-1, keepdims=True) + EPS)
    return (y * g.astype(jnp.float32)).astype(x.dtype)

def project_in(h, w_in, b_forget):
    z = h @ w_in
    splits = [WIDTH_A, 2 * WIDTH_A, 3 * WIDTH_A, 3 * WIDTH_A + N_HEADS_A,
              3 * WIDTH_A + N_HEADS_A + WIDTH_B, 3 * WIDTH_A + N_HEADS_A + 2 * WIDTH_B]
    qa, ka, va, fa, qb, kb, vb = jnp.split(z, splits, axis=-1)
    heads = lambda t, n: t.reshape(t.shape[:-1] + (n, HEAD_DIM))
    logf = jax.nn.log_sigmoid((fa + b_forget).astype(jnp.float32))
    return (heads(qa, N_HEADS_A), heads(ka, N_HEADS_A), heads(va, N_HEADS_A), logf,
            heads(qb, N_HEADS_B), heads(kb, N_HEADS_B), heads(vb, N_HEADS_B))

def attend(q, k, v, bias, valid):
    s = jnp.einsum('bqhd,bkhd->bhqk', q, k).astype(jnp.float32) * SCALE + bias
    s = jnp.where(valid, s, -jnp.inf)
    p = jax.nn.softmax(s, axis=-1)
    return jnp.einsum('bhqk,bkhd->bqhd', p.astype(v.dtype), v)

def rel_bias_matrix(rel_bias, dist):
    idx = jnp.clip(dist, -REL_CLIP, REL_CLIP) + REL_CLIP
    return rel_bias[:, idx].astype(jnp.float32)

def fox_prompt(q, k, v, logf):
    b, s = q.shape[0], q.shape[1]
    nb = s // Q_BLOCK
    c = jnp.cumsum(logf, axis=1).transpose(0, 2, 1)
    q_blocks = q.reshape(b, nb, Q_BLOCK, N_HEADS_A, HEAD_DIM).transpose(1, 0, 2, 3, 4)
    c_blocks = c.reshape(b, N_HEADS_A, nb, Q_BLOCK).transpose(2, 0, 1, 3)
    spos = jnp.arange(s)

    def one_block(args):
        qb_, cq, blk = args
        tpos = blk * Q_BLOCK + jnp.arange(Q_BLOCK)
        bias = cq[..., :, None] - c[..., None, :]
        valid = spos[None, :] <= tpos[:, None]
        return attend(qb_, k, v, bias, valid)

    out = lax.map(one_block, (q_blocks, c_blocks, jnp.arange(nb)))
    return out.transpose(1, 0, 2, 3, 4).reshape(b, s, N_HEADS_A, HEAD_DIM)

def fox_sample(q, k, v, logf, cache_k, cache_v, cache_logf):
    p_len, t_len = cache_k.shape[1], q.shape[1]
    k_all = jnp.concatenate([cache_k, k], axis=1)
    v_all = jnp.concatenate([cache_v, v], axis=1)
    c = jnp.cumsum(jnp.concatenate([cache_logf.astype(jnp.float32), logf], axis=1), axis=1)
    c = c.transpose(0, 2, 1)
    bias = c[..., p_len:, None] - c[..., None, :]
    valid = jnp.arange(p_len + t_len)[None, :] <= (p_len + jnp.arange(t_len))[:, None]
    return attend(q, k_all, v_all, bias, valid)

def band_prompt(q, k, v, rel_bias):
    b, s = q.shape[0], q.shape[1]
    nc = s // CHUNK
    pad = ((0, 0), (LEFT_REACH, 0), (0, 0), (0, 0))
    kp, vp = jnp.pad(k, pad), jnp.pad(v, pad)
    i = jnp.arange(CHUNK)
    j = jnp.arange(BAND)
    bias = rel_bias_matrix(rel_bias, i[:, None] + LEFT_REACH - j[None, :])

    def one_chunk(ci):
        start = ci * CHUNK
        qc = lax.dynamic_slice_in_dim(q, start, CHUNK, axis=1)
        kband = lax.dynamic_slice_in_dim(kp, start, BAND, axis=1)
        vband = lax.dynamic_slice_in_dim(vp, start, BAND, axis=1)
        valid = (start + j - LEFT_REACH) >= 0
        return attend(qc, kband, vband, bias, valid[None, :])

    out = lax.map(one_chunk, jnp.arange(nc))
    return out.transpose(1, 0, 2, 3, 4).reshape(b, s, N_HEADS_B, HEAD_DIM)

def band_sample(q, k, v, rel_bias, cache_k, cache_v):
    l_len, t_len = cache_k.shape[1], q.shape[1]
    k_all = jnp.concatenate([cache_k, k], axis=1)
    v_all = jnp.concatenate([cache_v, v], axis=1)
    dist = jnp.arange(t_len)[:, None] + l_len - jnp.arange(l_len + t_len)[None, :]
    bias = rel_bias_matrix(rel_bias, dist)
    return attend(q, k_all, v_all, bias, True)

def trunk_layer(x, fox_fn, band_fn, norm_mix_pre, w_in, b_forget, gain_out_a, gain_out_b,
                w_out, norm_mix_post, norm_ffn_pre, w_gate, w_up, w_down, norm_ffn_post):
    h = rmsnorm(x, norm_mix_pre)
    qa, ka, va, logf, qb, kb, vb = project_in(h, w_in, b_forget)
    oa = fox_fn(qa, ka, va, logf)
    ob = band_fn(qb, kb, vb)
    oa = rmsnorm(oa.reshape(oa.shape[:-2] + (WIDTH_A,)), gain_out_a)
    ob = rmsnorm(ob.reshape(ob.shape[:-2] + (WIDTH_B,)), gain_out_b)
    mix = jnp.concatenate([oa, ob], axis=-1) @ w_out
    x = x + rmsnorm(mix, norm_mix_post)
    hf = rmsnorm(x, norm_ffn_pre)
    ff = (jax.nn.silu(hf @ w_gate) * (hf @ w_up)) @ w_down
    x = x + rmsnorm(ff, norm_ffn_post)
    return x, (ka, va, logf, kb, vb)

def setup_inputs(seed: int = 0) -> dict:
    key = jax.random.key(seed)
    ks = jax.random.split(key, 20)
    nrm = jax.random.normal
    f32 = jnp.float32
    b_len = min(LEFT_REACH, PAST_LEN)
    gain = lambda k, n: 1.0 + 0.05 * nrm(k, (DEPTH, n), f32)
    return {
        "x_prompt": nrm(ks[0], (BATCH, SEQ, D_MODEL), f32),
        "x_sample": nrm(ks[1], (DEC_BATCH, DEC_SEQ, D_MODEL), f32),
        "cache_a_k": nrm(ks[2], (DEPTH, DEC_BATCH, PAST_LEN, N_HEADS_A, HEAD_DIM), f32),
        "cache_a_v": nrm(ks[3], (DEPTH, DEC_BATCH, PAST_LEN, N_HEADS_A, HEAD_DIM), f32),
        "cache_a_logf": jax.nn.log_sigmoid(4.0 + nrm(ks[4], (DEPTH, DEC_BATCH, PAST_LEN, N_HEADS_A), f32)),
        "cache_b_k": nrm(ks[5], (DEPTH, DEC_BATCH, b_len, N_HEADS_B, HEAD_DIM), f32),
        "cache_b_v": nrm(ks[6], (DEPTH, DEC_BATCH, b_len, N_HEADS_B, HEAD_DIM), f32),
        "norm_mix_pre": gain(ks[7], D_MODEL),
        "w_in": nrm(ks[8], (DEPTH, D_MODEL, D_IN), f32) * D_MODEL ** -0.5,
        "b_forget": 4.0 + 0.5 * nrm(ks[9], (DEPTH, N_HEADS_A), f32),
        "rel_bias": 0.1 * nrm(ks[10], (DEPTH, N_HEADS_B, 2 * REL_CLIP + 1), f32),
        "gain_out_a": gain(ks[11], WIDTH_A),
        "gain_out_b": gain(ks[12], WIDTH_B),
        "w_out": nrm(ks[13], (DEPTH, MIX_WIDTH, D_MODEL), f32) * MIX_WIDTH ** -0.5,
        "norm_mix_post": gain(ks[14], D_MODEL),
        "norm_ffn_pre": gain(ks[15], D_MODEL),
        "w_gate": nrm(ks[16], (DEPTH, D_MODEL, D_FF), f32) * D_MODEL ** -0.5,
        "w_up": nrm(ks[17], (DEPTH, D_MODEL, D_FF), f32) * D_MODEL ** -0.5,
        "w_down": nrm(ks[18], (DEPTH, D_FF, D_MODEL), f32) * D_FF ** -0.5,
        "norm_ffn_post": gain(ks[19], D_MODEL),
    }

def reference(x_prompt, x_sample, cache_a_k, cache_a_v, cache_a_logf, cache_b_k, cache_b_v,
              norm_mix_pre, w_in, b_forget, rel_bias, gain_out_a, gain_out_b, w_out,
              norm_mix_post, norm_ffn_pre, w_gate, w_up, w_down, norm_ffn_post):
    xp, xs = x_prompt, x_sample
    keep = min(LEFT_REACH, x_prompt.shape[1])
    pa_k, pa_v, pa_f, pb_k, pb_v = [], [], [], [], []
    sa_k, sa_v, sa_f, sb_k, sb_v = [], [], [], [], []
    for l in range(DEPTH):
        weights = (norm_mix_pre[l], w_in[l], b_forget[l], gain_out_a[l], gain_out_b[l], w_out[l],
                   norm_mix_post[l], norm_ffn_pre[l], w_gate[l], w_up[l], w_down[l], norm_ffn_post[l])
        xp, (ka, va, lf, kb, vb) = trunk_layer(
            xp, fox_prompt, functools.partial(band_prompt, rel_bias=rel_bias[l]), *weights)
        pa_k.append(ka); pa_v.append(va); pa_f.append(lf)
        pb_k.append(kb[:, kb.shape[1] - keep:]); pb_v.append(vb[:, vb.shape[1] - keep:])
        xs, (ka, va, lf, kb, vb) = trunk_layer(
            xs,
            functools.partial(fox_sample, cache_k=cache_a_k[l], cache_v=cache_a_v[l], cache_logf=cache_a_logf[l]),
            functools.partial(band_sample, rel_bias=rel_bias[l], cache_k=cache_b_k[l], cache_v=cache_b_v[l]),
            *weights)
        sa_k.append(ka); sa_v.append(va); sa_f.append(lf); sb_k.append(kb); sb_v.append(vb)
    st = jnp.stack
    return (xp, xs, st(pa_k), st(pa_v), st(pa_f), st(pb_k), st(pb_v),
            st(sa_k), st(sa_v), st(sa_f), st(sb_k), st(sb_v))


_drawn_inputs = setup_inputs


def setup_inputs(seed=0):
    import zlib

    import numpy as np

    out = dict(_drawn_inputs(seed))
    spreads = {}
    factors = {}
    for name, (base, spread) in spreads.items():
        noise = np.random.default_rng([zlib.crc32(name.encode()), seed]).standard_normal(out[name].shape)
        drawn = base * np.exp(spread * noise) if base else spread * noise
        out[name] = __import__('jax').numpy.asarray(drawn.astype(out[name].dtype))
    for name, factor in factors.items():
        out[name] = (out[name] * factor).astype(out[name].dtype)
    return out
```

```python
import concourse.bass as bass
from concourse import mybir
from contextlib import ExitStack

F32 = mybir.dt.float32
F32R = mybir.dt.float32r
ALU = mybir.AluOpType
ACT = mybir.ActivationFunctionType
AX = mybir.AxisListType
RMAX = bass.bass_isa.ReduceOp.max
ds = bass.ds

P = 128
D = 1024
KD = D // P
SEQ = 2048
NB, NQ = 8, 16
PAST_A, PAST_B = 1024, 512
TOK = SEQ + NB * NQ
NT = TOK // P
H, HD = 8, 64
GW = H * HD
FF = 2816
NJ = FF // P
EPS = 1e-6
SCALE = HD ** -0.5
NEG = -1.0e30
CLIP = 128
TBLK = [(0, 448), (448, 448), (896, 448), (1344, 448), (1792, 384)]


def f32(ap):
    return ap.bitcast(F32)


class Mem:

    def __init__(self, nc, ctx, tag):
        self.nc, self.ctx, self.tag, self.sems = nc, ctx, tag, []

    def sb(self, name, shape, dt=F32):
        return self.ctx.enter_context(self.nc.sbuf_tensor(f"{self.tag}_{name}", shape, dt))

    def ps(self, name, shape):
        return self.ctx.enter_context(self.nc.psum_tensor(f"{self.tag}_{name}", shape, F32))

    def sem(self, name):
        s = self.ctx.enter_context(self.nc.semaphore(f"{self.tag}_{name}"))
        self.sems.append(s)
        return s

    def clear_sems(self):
        with self.nc.Block() as block:

            @block.gpsimd
            def _(pool):
                for s in self.sems:
                    pool.sem_clear(s)


def norm_inputs(nc, t, xhi, xlo):
    with ExitStack() as ctx:
        m = Mem(nc, ctx, "nrm")
        W = 448
        x = [m.sb(f"x{u}", [P, KD, W]) for u in range(2)]
        sq = [m.sb(f"sq{u}", [P, W]) for u in range(2)]
        acc = m.sb("acc", [P, W])
        var = m.sb("var", [P, W])
        rstd = m.sb("rstd", [P, W])
        ones = m.sb("ones", [P, P])
        gain = m.sb("gain", [P, KD])
        tot = m.ps("tot", [P, 512])
        s_x = [m.sem(f"s_x{u}") for u in range(2)]
        s_gain, s_ones, s_sq, s_acc, s_tot, s_var, s_std, s_rstd, s_xn, s_hi, s_lo = (
            m.sem(n) for n in ("gain", "ones", "sq", "acc", "tot", "var", "std", "rstd", "xn", "hi", "lo"))
        with nc.Block() as block:

            @block.sync
            def _(sp):
                sp.dma_start(gain[:], t["g_pre"]).then_inc(s_gain, 16)
                for b, (t0, w) in enumerate(TBLK):
                    if b >= 2:
                        sp.wait_ge(s_lo, b - 1)
                    sp.dma_start(x[b % 2][:, :, :w], t["xT"][:, :, t0:t0 + w]).then_inc(s_x[b % 2], 16)
                sp.wait_ge(s_lo, len(TBLK))

            @block.scalar
            def _(act):
                for b, (t0, w) in enumerate(TBLK):
                    act.wait_ge(s_x[b % 2], 16 * (b // 2 + 1))
                    for k in range(KD):
                        n = b * KD + k
                        if n >= 2:
                            act.wait_ge(s_acc, n - 1)
                        nc.scalar.activation(sq[n % 2][:, :w], x[b % 2][:, k, :w], ACT.Square).then_inc(s_sq, 1)
                    act.wait_ge(s_var, b + 1)
                    nc.scalar.activation(var[:, :w], var[:, :w], ACT.Sqrt).then_inc(s_std, 1)
                    for k in range(KD):
                        act.wait_ge(s_xn, b * KD + k + 1)
                        last = nc.scalar.activation(xhi[:, k, t0:t0 + w], x[b % 2][:, k, :w], ACT.Copy)
                        last.then_inc(s_hi, 1)

            @block.gpsimd
            def _(pool):
                for b, (t0, w) in enumerate(TBLK):
                    for k in range(KD):
                        n = b * KD + k
                        pool.wait_ge(s_sq, n + 1)
                        if k == 0:
                            if b >= 1:
                                pool.wait_ge(s_tot, b)
                            nc.gpsimd.tensor_copy(acc[:, :w], sq[n % 2][:, :w]).then_inc(s_acc, 1)
                        else:
                            pool.wait_ge(s_acc, n)
                            nc.gpsimd.tensor_tensor(acc[:, :w], acc[:, :w], sq[n % 2][:, :w], ALU.add).then_inc(s_acc, 1)

            @block.tensor
            def _(pe):
                pe.wait_ge(s_ones, 1)
                for b, (t0, w) in enumerate(TBLK):
                    pe.wait_ge(s_acc, (b + 1) * KD)
                    if b >= 1:
                        pe.wait_ge(s_var, b)
                    nc.tensor.matmul(tot[:, :w], ones[:], acc[:, :w], start=True, stop=True).then_inc(s_tot, 1)

            @block.vector
            def _(dve):
                nc.vector.memset(ones[:], 1.0).then_inc(s_ones, 1)
                dve.wait_ge(s_gain, 16)
                for b, (t0, w) in enumerate(TBLK):
                    dve.wait_ge(s_tot, b + 1)
                    nc.vector.tensor_scalar(var[:, :w], tot[:, :w], 1.0 / D, EPS, ALU.mult, ALU.add).then_inc(s_var, 1)
                    dve.wait_ge(s_std, b + 1)
                    nc.vector.reciprocal(rstd[:, :w], var[:, :w]).then_inc(s_rstd, 1)
                    dve.wait_ge(s_rstd, b + 1)
                    for k in range(KD):
                        nc.vector.scalar_tensor_tensor(x[b % 2][:, k, :w], x[b % 2][:, k, :w], gain[:, k:k + 1], rstd[:, :w],
                                                       ALU.mult, ALU.mult).then_inc(s_xn, 1)
                    for k in range(KD):
                        dve.wait_ge(s_hi, b * KD + k + 1)
                        last = nc.vector.tensor_tensor(xlo[:, k, t0:t0 + w], x[b % 2][:, k, :w], f32(xhi[:, k, t0:t0 + w]),
                                                       ALU.subtract)
                    last.then_inc(s_lo, 1)


def pairs(eng, n, body):
    body(0)
    with eng.Fori(1, n) as i:
        body(i)


def after(eng, sem, value):
    if not isinstance(value, int) or value > 0:
        eng.wait_ge(sem, value)


def three(nc, out, kk, a_hi, a_lo, b_hi, b_lo):
    for k in range(kk):
        nc.tensor.matmul(out, a_hi(k), b_hi(k), start=(k == 0), stop=False)
        nc.tensor.matmul(out, a_hi(k), b_lo(k), start=False, stop=False)
        last = nc.tensor.matmul(out, a_lo(k), b_hi(k), start=False, stop=(k == kk - 1))
    return last


def project_in(nc, t, xhi, xlo):
    CW = 256
    NZ, NV = 4 * GW // CW, 2 * GW // CW
    NS, NBK = NZ + NV, len(TBLK)
    with ExitStack() as ctx:
        m = Mem(nc, ctx, "prj")
        raw = [m.sb(f"raw{u}", [P, KD, CW]) for u in range(2)]
        hi = [m.sb(f"hi{u}", [P, KD, CW], F32R) for u in range(2)]
        lo = [m.sb(f"lo{u}", [P, KD, CW], F32R) for u in range(2)]
        zo = [m.sb(f"zo{u}", [P, 448]) for u in range(NBK)]
        vo = [m.sb(f"vo{u}", [P, CW]) for u in range(2)]
        wf = m.sb("wf", [P, KD, H])
        wfh = m.sb("wfh", [P, KD, H], F32R)
        wfl = m.sb("wfl", [P, KD, H], F32R)
        pz = [m.ps(f"pz{u}", [P, 512]) for u in range(NBK)]
        pv = [m.ps(f"pv{u}", [P, 512]) for u in range(2)]
        s_raw = [m.sem(f"raw{u}") for u in range(2)]
        s_zs = [m.sem(f"z_stored{u}") for u in range(NBK)]
        s_vs = [m.sem(f"v_stored{u}") for u in range(2)]
        s_wf, s_hi, s_lo, s_z, s_ze, s_v, s_ve = (m.sem(n) for n in ("wf", "hi", "lo", "z", "ze", "v", "ve"))

        def slab_done(eng, s):
            if s < NZ:
                eng.wait_ge(s_z, (s + 1) * 2 * NBK)
            else:
                eng.wait_ge(s_v, (s - NZ + 1) * NT)

        with nc.Block() as block:

            @block.sync
            def _(sp):
                sp.dma_start(wf[:], t["w_f"]).then_inc(s_wf, 16)
                for s in range(NS):
                    if s >= 2:
                        sp.wait_ge(s_lo, s - 1 + 1)
                    sp.dma_start(raw[s % 2][:], t["w_slab"][s]).then_inc(s_raw[s % 2], 16)

            @block.gpsimd
            def _(pool):
                pool.wait_ge(s_wf, 16)
                nc.gpsimd.tensor_copy(wfh[:], wf[:]).then_inc(s_hi, 1)
                for s in range(NS):
                    pool.wait_ge(s_raw[s % 2], 16 * (s // 2 + 1))
                    if s >= 2:
                        slab_done(pool, s - 2)
                    nc.gpsimd.tensor_copy(hi[s % 2][:], raw[s % 2][:]).then_inc(s_hi, 1)

            @block.vector
            def _(dve):
                dve.wait_ge(s_hi, 1)
                nc.vector.tensor_tensor(wfl[:], wf[:], f32(wfh[:]), ALU.subtract).then_inc(s_lo, 1)
                for s in range(NS):
                    dve.wait_ge(s_hi, s + 2)
                    if s >= 2:
                        slab_done(dve, s - 2)
                    nc.vector.tensor_tensor(lo[s % 2][:], raw[s % 2][:], f32(hi[s % 2][:]), ALU.subtract).then_inc(s_lo, 1)

            @block.tensor
            def _(pe):
                def z_pair(i):
                    for u in range(2):
                        pe.wait_ge(s_lo, 2 * i + u + 2)
                        for c in range(2):
                            for b, (t0, w) in enumerate(TBLK):
                                n = ((2 * i + u) * 2 + c) * NBK + b
                                after(pe, s_ze, n - NBK + 1)
                                three(nc, pz[b][:, :w], KD,
                                      lambda k: hi[u][:, k, c * P:(c + 1) * P], lambda k: lo[u][:, k, c * P:(c + 1) * P],
                                      lambda k: xhi[:, k, t0:t0 + w], lambda k: xlo[:, k, t0:t0 + w]).then_inc(s_z, 1)

                def v_slab(s, u):
                    pe.wait_ge(s_lo, s + NZ + 2)
                    for c in range(NT):
                        n = s * NT + c
                        after(pe, s_ve, n - 1)
                        three(nc, pv[n % 2][:, :CW], KD,
                              lambda k: xhi[:, k, c * P:(c + 1) * P], lambda k: xlo[:, k, c * P:(c + 1) * P],
                              lambda k: hi[u][:, k, :], lambda k: lo[u][:, k, :]).then_inc(s_v, 1)

                pairs(pe, NZ // 2, z_pair)
                for s in range(NV):
                    v_slab(s, s % 2)
                pe.wait_ge(s_lo, 1)
                for b, (t0, w) in enumerate(TBLK):
                    pe.wait_ge(s_ze, (2 * NZ - 1) * NBK + b + 1)
                    three(nc, pz[b][:H, :w], KD,
                          lambda k: wfh[:, k, :], lambda k: wfl[:, k, :],
                          lambda k: xhi[:, k, t0:t0 + w], lambda k: xlo[:, k, t0:t0 + w]).then_inc(s_z, 1)

            @block.scalar
            def _(act):
                def z_pair(i):
                    for u in range(2):
                        for c in range(2):
                            g = (2 * i + u) * 2 + c
                            for b, (t0, w) in enumerate(TBLK):
                                act.wait_ge(s_z, g * NBK + b + 1)
                                after(act, s_zs[b], 16 * g)
                                nc.scalar.activation(zo[b][:, :w], pz[b][:, :w], ACT.Copy).then_inc(s_ze, 1)
                                act.wait_ge(s_ze, g * NBK + b + 1)
                                act.dma_start(t["zT"][ds(g * P, P), t0:t0 + w], zo[b][:, :w]).then_inc(s_zs[b], 16)

                pairs(act, NZ // 2, z_pair)
                for s in range(NV):
                    for c in range(NT):
                        n = s * NT + c
                        act.wait_ge(s_v, n + 1)
                        after(act, s_vs[n % 2], 16 * (n // 2))
                        nc.scalar.activation(vo[n % 2][:], pv[n % 2][:, :CW], ACT.Copy).then_inc(s_ve, 1)
                        act.wait_ge(s_ve, n + 1)
                        act.dma_start(t["v"][c * P:(c + 1) * P, s * CW:(s + 1) * CW], vo[n % 2][:]).then_inc(s_vs[n % 2], 16)
                for b, (t0, w) in enumerate(TBLK):
                    act.wait_ge(s_z, 2 * NZ * NBK + b + 1)
                    act.wait_ge(s_zs[b], 16 * 2 * NZ)
                    nc.scalar.activation(zo[b][:H, :w], pz[b][:H, :w], ACT.Copy).then_inc(s_ze, 1)
                    act.wait_ge(s_ze, 2 * NZ * NBK + b + 1)
                    act.dma_start(t["fT"][:, t0:t0 + w], zo[b][:H, :w]).then_inc(s_zs[b], 16)
                for b in range(NBK):
                    act.wait_ge(s_zs[b], 16 * (2 * NZ + 1))
                for u in range(2):
                    act.wait_ge(s_vs[u], 16 * (NV * NT // 2))


def forget(nc, t, neg_c):
    L = PAST_A + NQ
    with ExitStack() as ctx:
        m = Mem(nc, ctx, "fgt")
        z = m.sb("z", [H, TOK])
        e = m.sb("e", [H, TOK])
        w = m.sb("w", [H, TOK])
        d = m.sb("d", [H, TOK])
        lf = m.sb("lf", [H, TOK])
        cp = m.sb("cp", [H, SEQ])
        cs = m.sb("cs", [NB * H, L])
        css = m.sb("css", [NB * H, L])
        bf = m.sb("bf", [H, 1])
        eye = m.sb("eye", [H, H])
        pc = m.ps("pc", [P, 512])
        s_in, s_sm, s_lf, s_out, s_eye, s_st, s_pe = (m.sem(n) for n in ("in", "sm", "lf", "out", "eye", "st", "pe"))
        s_act = m.sem("act")
        with nc.Block() as block:

            @block.sync
            def _(sp):
                sp.dma_start(z[:], t["fT"]).then_inc(s_in, 16)
                sp.dma_start(bf[:], t["b_forget"]).then_inc(s_in, 16)
                sp.dma_start(cs[:, 0:PAST_A], t["cache_logf"]).then_inc(s_in, 16)
                sp.wait_ge(s_st, 10)
                sp.dma_start(t["lfT"], lf[:]).then_inc(s_lf, 16)
                sp.wait_ge(s_lf, 16)
                for b in range(NB):
                    sp.dma_start(cs[b * H:(b + 1) * H, PAST_A:], t["lfT"][:, SEQ + b * NQ:SEQ + (b + 1) * NQ]).then_inc(s_sm, 16)
                sp.wait_ge(s_st, 12)
                sp.dma_start(t["csum"], css[:]).then_inc(s_out, 16)
                sp.wait_ge(s_out, 16)

            @block.gpsimd
            def _(pool):
                nc.gpsimd.memset(eye[:], 0.0).then_inc(s_eye, 1)
                pool.wait_ge(s_eye, 1)
                nc.gpsimd.affine_select(out=eye[:], in_=eye[:], compare_op=ALU.not_equal, fill=1.0, base=0,
                                        pattern=[[-1, H]], channel_multiplier=1).then_inc(s_eye, 1)

            @block.scalar
            def _(act):
                act.wait_ge(s_st, 2)
                nc.scalar.activation(e[:], e[:], ACT.Exp).then_inc(s_act, 1)
                act.wait_ge(s_st, 3)
                nc.scalar.activation(lf[:], w[:], ACT.Ln).then_inc(s_act, 1)

            @block.vector
            def _(dve):
                n = [0]

                def step(ins):
                    n[0] += 1
                    ins.then_inc(s_st, 1)
                    dve.wait_ge(s_st, n[0])

                dve.wait_ge(s_in, 48)
                step(nc.vector.tensor_scalar(z[:], z[:], bf[:, 0:1], None, ALU.add))
                step(nc.vector.scalar_tensor_tensor(e[:], z[:], -1.0, z[:], ALU.mult, ALU.min))
                dve.wait_ge(s_act, 1)
                step(nc.vector.tensor_scalar(w[:], e[:], 1.0, None, ALU.add))
                step(nc.vector.tensor_scalar(d[:], w[:], -1.0, -1.0, ALU.add, ALU.mult))
                step(nc.vector.tensor_tensor(d[:], d[:], e[:], ALU.add))
                dve.wait_ge(s_act, 2)
                step(nc.vector.reciprocal(w[:], w[:]))
                step(nc.vector.tensor_tensor(d[:], d[:], w[:], ALU.mult))
                step(nc.vector.tensor_tensor(lf[:], lf[:], d[:], ALU.add))
                step(nc.vector.tensor_scalar(z[:], z[:], 0.0, None, ALU.min))
                step(nc.vector.tensor_tensor(lf[:], z[:], lf[:], ALU.subtract))
                step(nc.vector.tensor_tensor_scan(cp[:], lf[:, 0:SEQ], lf[:, 0:SEQ], 0.0, ALU.add, ALU.bypass))
                dve.wait_ge(s_sm, 16 * NB)
                step(nc.vector.tensor_tensor_scan(css[:], cs[:], cs[:], 0.0, ALU.add, ALU.bypass))
                dve.wait_ge(s_pe, 1)
                step(nc.vector.tensor_scalar(neg_c[:], pc[:, 0:SEQ // P * H].rearrange("p (a h) -> p a h", h=H), -1.0, None,
                                             ALU.mult))

            @block.tensor
            def _(pe):
                pe.wait_ge(s_st, 11)
                pe.wait_ge(s_eye, 2)
                for a in range(SEQ // P):
                    last = nc.tensor.matmul(pc[:, a * H:(a + 1) * H], cp[:, a * P:(a + 1) * P], eye[:], start=True, stop=True)
                last.then_inc(s_pe, 1)


def rel_tables(nc, t, dhi, dlo, m_fox, m_old, cols, neg_c):
    EXT = 3 * P
    with ExitStack() as ctx:
        m = Mem(nc, ctx, "tab")
        rb = m.sb("rb", [H, 2 * CLIP + 1])
        ext = m.sb("ext", [H, EXT])
        far = m.sb("far", [P, H])
        near = m.sb("near", [P, H, 2 * P])
        chunk = m.sb("chunk", [P, 2 * P])
        caus = m.sb("caus", [P, 2 * P])
        old = m.sb("old", [P, 2 * P])
        s_in, s_ext, s_sk, s_far, s_near, s_m, s_v = (m.sem(n) for n in ("in", "ext", "sk", "far", "near", "m", "v"))
        with nc.Block() as block:

            @block.sync
            def _(sp):
                sp.dma_start(rb[:], t["rel_bias"]).then_inc(s_in, 16)
                rbd = t["rel_bias"]
                sp.dma_start(far[:], bass.AP(rbd.tensor, rbd.offset + 2 * CLIP, [[0, P], [2 * CLIP + 1, H]]),
                             allow_slow_non_contiguous=True).then_inc(s_far, 16)
                sp.wait_ge(s_v, 2)
                for p in range(0, P, 16):
                    sp.dma_start(t["skew"][:, p:p + 16, :], ext[:, None, :].to_broadcast([H, 16, EXT])).then_inc(s_sk, 16)
                sp.wait_ge(s_sk, 16 * (P // 16))
                sk = t["skew"]
                for h in range(H):
                    walk = bass.AP(sk.tensor, sk.offset + h * P * EXT + P - 1, [[EXT - 1, P], [1, 2 * P]])
                    sp.dma_start(near[:, h, :], walk).then_inc(s_near, 16)

            @block.vector
            def _(dve):
                dve.wait_ge(s_in, 16)
                nc.vector.tensor_copy(ext[:, 0:2 * CLIP], rb[:, 1:]).then_inc(s_v, 1)
                nc.vector.tensor_copy(ext[:, 2 * CLIP:], rb[:, 2 * CLIP:].to_broadcast([H, EXT - 2 * CLIP])).then_inc(s_v, 1)
                dve.wait_ge(s_far, 16)
                nc.vector.tensor_copy(cols[:, 0:H, :], neg_c[:].rearrange("p a h -> p h a"))
                nc.vector.tensor_copy(cols[:, H:2 * H, :], far[:, :, None].to_broadcast([P, H, SEQ // P]))
                dve.wait_ge(s_near, 16 * H)
                dve.wait_ge(s_m, 6)
                for h in range(H):
                    nc.vector.scalar_tensor_tensor(near[:, h, :], near[:, h, :], far[:, h:h + 1], chunk[:], ALU.subtract,
                                                   ALU.add).then_inc(s_v, 1)
                nc.vector.tensor_copy(m_fox[:], caus[:])
                nc.vector.tensor_copy(m_old[:], old[:])
                dve.wait_ge(s_v, 2 + H)
                nc.vector.tensor_copy(dhi[:], near[:]).then_inc(s_v, 1)
                dve.wait_ge(s_v, 3 + H)
                nc.vector.tensor_tensor(dlo[:], near[:], f32(dhi[:]), ALU.subtract).then_inc(s_v, 1)

            @block.gpsimd
            def _(pool):
                for tile in (chunk, caus, old):
                    nc.gpsimd.memset(tile[:], 0.0).then_inc(s_m, 1)
                pool.wait_ge(s_m, 3)
                nc.gpsimd.affine_select(out=caus[:, 0:P], in_=caus[:, 0:P], compare_op=ALU.is_ge, fill=NEG, base=0,
                                        pattern=[[1, P]], channel_multiplier=-1).then_inc(s_m, 1)
                pool.wait_ge(s_m, 4)
                nc.gpsimd.memset(chunk[64:128, 0:64], NEG).then_inc(s_m, 1)
                pool.wait_ge(s_m, 5)
                nc.gpsimd.memset(old[0:64, P + 64:2 * P], NEG).then_inc(s_m, 1)


QG = 512
NG = SEQ // QG


def units(band, g):
    out = []
    tiles = range(max(0, 4 * g - 4) if band else 0, 4 * g + 4)
    for kt in [4 * g] + [k for k in tiles if k != 4 * g]:
        i0, i1 = max(kt, 4 * g), min(kt + 4, 4 * g + 3) if band else 4 * g + 3
        w = (i1 - i0 + 1) * P
        adds = []
        if kt >= 4 * g:
            adds.append(("near" if band else "fox", 0, 0, min(w, 2 * P)))
        elif band and kt == 4 * g - 1:
            adds.append(("near", P, 0, P))
        if band and kt < 4 * g:
            wide = min(w, 2 * P)
            adds.append(("old", 2 * P - wide, w - wide, wide))
        out.append((kt, (i0 - 4 * g) * P, w, adds))
    return out


def merged(n_exp, n_max):
    lead = max(n_exp - 5, 1)
    out = []
    for e in range(n_exp):
        if e < lead:
            out += [("M", j) for j in range(n_max * e // lead, n_max * (e + 1) // lead)]
        out.append(("E", e))
    return out


def attend_prompt(nc, t, dhi, dlo, m_fox, m_old, cols):
    NP = 4
    U = {band: [units(band, g) for g in range(NG)] for band in (False, True)}
    start = {band: [sum(len(x) for x in U[band][:g]) for g in range(NG + 1)] for band in (False, True)}
    NU = {band: start[band][NG] for band in (False, True)}
    assert all(n % NP == 0 for n in NU.values())

    def unit0(band, h):
        return H * NU[False] + h * NU[True] if band else h * NU[False]

    with ExitStack() as ctx:
        m = Mem(nc, ctx, "att")
        kd = m.sb("kd", [P, SEQ])
        qd = m.sb("qd", [P, SEQ])
        vr = m.sb("vr", [P, SEQ // P, HD])
        K1 = [m.sb(f"k1{u}", [P, SEQ], F32R) for u in range(2)]
        K2 = [m.sb(f"k2{u}", [P, SEQ], F32R) for u in range(2)]
        Q1 = [m.sb(f"q1{u}", [P, SEQ], F32R) for u in range(2)]
        Q2 = [m.sb(f"q2{u}", [P, SEQ], F32R) for u in range(2)]
        VA = [m.sb(f"va{u}", [P, SEQ // P, 2 * HD], F32R) for u in range(2)]
        VB = [m.sb(f"vb{u}", [P, SEQ // P, 2 * HD], F32R) for u in range(2)]
        VC = m.sb("vc", [P, 2 * HD], F32R)
        col = [m.sb(f"col{u}", [P, SEQ // P]) for u in range(2)]
        eye = m.sb("eye", [P, P])
        eyeR = m.sb("eyer", [P, P], F32R)
        run = [m.sb(f"run{u}", [P, QG]) for u in range(2)]
        top = [m.sb(f"top{u}", [P, QG]) for u in range(2)]
        pr = [m.sb(f"pr{u}", [P, QG]) for u in range(NP)]
        ph = [m.sb(f"ph{u}", [P, QG], F32R) for u in range(NP)]
        pl = [m.sb(f"pl{u}", [P, QG], F32R) for u in range(NP)]
        f1 = m.sb("f1", [HD, QG])
        f2 = m.sb("f2", [HD, QG])
        f3 = m.sb("f3", [HD, QG])
        fr = m.sb("fr", [HD, QG])
        fo = [m.sb(f"fo{u}", [HD, QG]) for u in range(2)]
        sm = [m.ps(f"sm{u}", [P, QG]) for u in range(2)]
        se = [m.ps(f"se{u}", [P, QG]) for u in range(2)]
        oa = [m.ps(f"oa{u}", [P, QG]) for u in range(2)]
        ob = [m.ps(f"ob{u}", [P, QG]) for u in range(2)]
        table = {"fox": (m_fox, None), "old": (m_old, None), "near": (dhi, dlo)}
        (s_ld, s_cst, s_eye, s_pa, s_pq, s_pd, s_pp, s_mq, s_mx, s_ar, s_na, s_nm, s_eq, s_ex, s_hi, s_lo, s_pv, s_fc, s_fa,
         s_fr, s_fo, s_fs, s_tick) = (m.sem(n) for n in (
             "loaded", "consts", "eye", "k_high", "q_high", "split", "cleared", "max_scores", "max_taken", "reduced", "neg_high",
             "neg_low", "scores", "exp", "exp_high", "exp_low", "pv", "copied", "added", "recip", "summed", "scaled", "tick"))
        s_os = [m.sem(f"stored{u}") for u in range(2)]
        ND = 5

        def walk(eng, prep, head):
            prep(False, 0, 0)
            for band in (False, True):
                for i in (0, None, H // 2 - 1):
                    if i is None:
                        with eng.Fori(1, H // 2 - 1) as r:
                            for u in range(2):
                                head(band, 2 * r + u, u, False, False)
                    else:
                        for u in range(2):
                            head(band, 2 * i + u, u, not band and i == 0 and u == 0, i == H // 2 - 1 and u == 1)

        def following(band, h, last):
            return (band, h + 1) if not last else None if band else (True, 0)

        def hno(band, h):
            return h + H if band else h

        def n_pos(n):
            return not isinstance(n, int) or n >= 2

        def prev_end(band, h):
            if band and isinstance(h, int) and h < 2:
                return unit0(False, H - 2 + h) + NU[False]
            return unit0(band, h - 1)

        with nc.Block() as block:

            @block.sync
            def _(sp):
                def load(band, h, u):
                    n = hno(band, h)
                    q0, v0 = (2 * GW, GW) if band else (0, 0)
                    after(sp, s_pd, 5 * n)
                    for r in range(2):
                        sp.dma_start(kd[64 * r:64 * r + 64, :], t["zT"][ds(q0 + GW + h * HD, HD), 0:SEQ]).then_inc(s_ld, 16)
                        sp.dma_start(qd[64 * r:64 * r + 64, :], t["zT"][ds(q0 + h * HD, HD), 0:SEQ]).then_inc(s_ld, 16)
                    sp.dma_start(vr[:], t["v"][0:SEQ, ds(v0 + h * HD, HD)].rearrange("(a p) c -> p a c", p=P)).then_inc(s_ld, 16)

                def store(band, h, g):
                    st = 4 * hno(band, h) + g
                    sp.wait_ge(s_fs, st + 1)
                    base = GW if band else 0
                    sp.dma_start(t["mixT"][ds(base + h * HD, HD), g * QG:(g + 1) * QG], fo[g % 2][:]).then_inc(s_os[g % 2], 16)

                def head(band, h, u, first, last):
                    nxt = following(band, h, last)
                    if nxt:
                        load(*nxt, 1 - u)
                    for g in range(NG):
                        store(band, h, g)

                walk(sp, load, head)
                for u in range(2):
                    sp.wait_ge(s_os[u], 16 * (2 * H * NG // 2))

            @block.tensor
            def _(pe):
                def scores(out, band, h, u, g, unit, sem):
                    kt, c0, w, adds = unit
                    q0 = g * QG + c0
                    ks = slice(kt * P, (kt + 1) * P)
                    mm = [(out[:, :w], K1[u][:, ks], Q1[u][:, q0:q0 + w]), (out[:, :w], K2[u][:, ks], Q2[u][:, q0:q0 + w])]
                    for name, a, at, n in adds:
                        for part in table[name]:
                            if part is not None:
                                src = part[:, ds(h, 1), a:a + n].rearrange("p a c -> p (a c)") if name == "near" else part[:, a:a + n]
                                mm.append((out[:, at:at + n], eyeR[:], src))
                    for n, (o, w_, x) in enumerate(mm):
                        last = nc.tensor.matmul(o, w_, x, start=(n == 0), stop=(n == len(mm) - 1), skip_group_check=True)
                    last.then_inc(sem, 1)

                def max_unit(band, h, u, g, j):
                    n = unit0(band, h) + start[band][g] + j
                    after(pe, s_mx, n - 1)
                    scores(sm[j % 2], band, h, u, g, U[band][g][j], s_mq)

                def exp_unit(band, h, u, g, j):
                    n = unit0(band, h) + start[band][g] + j
                    if j == 0:
                        pe.wait_ge(s_nm, 4 * hno(band, h) + g + 1)
                    after(pe, s_ex, n - 1)
                    scores(se[j % 2], band, h, u, g, U[band][g][j], s_eq)

                def pv_unit(band, h, u, k):
                    g = max(x for x in range(NG) if start[band][x] <= k)
                    j = k - start[band][g]
                    n = unit0(band, h) + k
                    st = 4 * hno(band, h) + g
                    kt, c0, w, _ = U[band][g][j]
                    first, end = j == 0, j == len(U[band][g]) - 1
                    pe.wait_ge(s_lo, n + 1)
                    if first:
                        after(pe, s_fr, st - 1)
                        after(pe, s_fc, st - 1)
                    b = k % NP
                    nc.tensor.matmul(oa[g % 2][:, c0:c0 + w], VA[u][:, kt, :], ph[b][:, :w], start=first, stop=end, skip_group_check=True)
                    nc.tensor.matmul(ob[g % 2][:, c0:c0 + w], VB[u][:, kt, :], pl[b][:, :w], start=first, stop=False, skip_group_check=True)
                    nc.tensor.matmul(ob[g % 2][:, c0:c0 + w], VC[:], ph[b][:, :w], start=False, stop=end,
                                     skip_group_check=True).then_inc(s_pv, 1)

                LAG = 2

                def ready(band, h, u):
                    pe.wait_ge(s_pd, 5 * hno(band, h) + 5)
                    pe.wait_ge(s_pp, hno(band, h) + 1)

                def begin(band, h, u):
                    pe.wait_ge(s_cst, 1)
                    ready(band, h, u)
                    for j in range(len(U[band][0])):
                        max_unit(band, h, u, 0, j)

                def head(band, h, u, first, last):
                    nxt = following(band, h, last)
                    before = band and isinstance(h, int) and h == 0
                    for g in range(NG):
                        more = (band, h, u, g + 1) if g + 1 < NG else (*nxt, 1 - u, 0) if nxt else None
                        if more and g + 1 == NG:
                            ready(*more[:3])
                        for kind, j in merged(len(U[band][g]), len(U[more[0]][more[3]]) if more else 0):
                            if kind == "M":
                                max_unit(*more, j)
                                continue
                            exp_unit(band, h, u, g, j)
                            k = start[band][g] + j - LAG
                            if k >= 0:
                                pv_unit(band, h, u, k)
                            elif before:
                                pv_unit(False, H - 1, 1 - u, NU[False] + k)
                            elif not first:
                                pv_unit(band, h - 1, 1 - u, NU[band] + k)
                    if nxt is None:
                        for k in range(NU[band] - LAG, NU[band]):
                            pv_unit(band, h, u, k)

                walk(pe, begin, head)

            def negate(eng, band, h, u, g):
                st = 4 * hno(band, h) + g
                c = slice(g * QG, (g + 1) * QG)
                if eng == "act":
                    nc.scalar.wait_ge(s_ar, st + 1)
                    nc.scalar.activation(Q2[u][64:128, c], top[g % 2][64:128, :], ACT.Copy, scale=-1.0).then_inc(s_na, 1)
                else:
                    nc.vector.wait_ge(s_na, st + 1)
                    nc.vector.scalar_tensor_tensor(Q2[u][96:128, c], top[g % 2][96:128, :], -1.0, f32(Q2[u][96:128, c]),
                                                   ALU.mult, ALU.subtract).then_inc(s_nm, 1)

            @block.scalar
            def _(act):
                def prep_k(band, h, u):
                    n = hno(band, h)
                    act.wait_ge(s_ld, 16 * ND * (n + 1))
                    if n_pos(n):
                        act.wait_ge(s_pv, prev_end(band, h))
                    nc.scalar.activation(K1[u][:], kd[:], ACT.Copy).then_inc(s_pa, 1)

                def prep_q(band, h, u):
                    nc.scalar.activation(Q1[u][:], qd[:], ACT.Copy, scale=SCALE).then_inc(s_pq, 1)

                def finish(band, h, g):
                    st = 4 * hno(band, h) + g
                    act.wait_ge(s_pv, unit0(band, h) + start[band][g + 1])
                    after(act, s_fs, st)
                    nc.scalar.activation(f1[:], oa[g % 2][HD:P, :], ACT.Copy)
                    nc.scalar.activation(f2[:], ob[g % 2][0:HD, :], ACT.Copy).then_inc(s_fc, 1)

                def exps(band, h, u, g, j):
                    n = unit0(band, h) + start[band][g] + j
                    kt, c0, w, _ = U[band][g][j]
                    b = (start[band][g] + j) % NP
                    act.wait_ge(s_eq, n + 1)
                    after(act, s_lo, n - NP + 1)
                    nc.scalar.activation(pr[b][:, :w], se[j % 2][:, :w], ACT.Exp, bias=col[u][:, kt:kt + 1]).then_inc(s_ex, 1)
                    after(act, s_pv, n - NP + 1)
                    act.wait_ge(s_ex, n + 1)
                    nc.scalar.activation(ph[b][:, :w], pr[b][:, :w], ACT.Copy).then_inc(s_hi, 1)

                def begin(band, h, u):
                    prep_k(band, h, u)
                    prep_q(band, h, u)
                    negate("act", band, h, u, 0)

                def head(band, h, u, first, last):
                    nxt = following(band, h, last)
                    before = band and isinstance(h, int) and h == 0
                    for g in range(NG):
                        n_exp = len(U[band][g])
                        more = (band, h, u, g + 1) if g + 1 < NG else (*nxt, 1 - u, 0) if nxt else None
                        for j in range(n_exp):
                            if j == n_exp - 1 and more:
                                negate("act", *more)
                            exps(band, h, u, g, j)
                            if j == 2 and g > 0:
                                finish(band, h, g - 1)
                            elif j == 2 and before:
                                finish(False, H - 1, NG - 1)
                            elif j == 2 and not first:
                                finish(band, h - 1, NG - 1)
                            if g == 1 and nxt and j == 3:
                                prep_k(*nxt, 1 - u)
                            if g == 1 and nxt and j == 5:
                                prep_q(*nxt, 1 - u)
                    if nxt is None:
                        finish(band, h, NG - 1)

                walk(act, begin, head)

            @block.gpsimd
            def _(pool):
                def settled():
                    pool.sem_inc(s_tick, 1)

                def clear(band, h, u):
                    n = hno(band, h)
                    if n_pos(n):
                        pool.wait_ge(s_pv, prev_end(band, h))
                    settled()
                    nc.gpsimd.memset(Q2[u][64:128, :].bitcast(F32), 0.0).then_inc(s_pp, 1)
                    pool.wait_ge(s_pp, n + 1)

                def reduce(band, h, u, g):
                    st = 4 * hno(band, h) + g
                    pool.wait_ge(s_mx, unit0(band, h) + start[band][g + 1])
                    after(pool, s_nm, st - 1)
                    settled()
                    nc.gpsimd.partition_all_reduce(top[g % 2][:], run[g % 2][:], P, RMAX).then_inc(s_ar, 1)
                    pool.wait_ge(s_ar, st + 1)

                def finish(band, h, g):
                    st = 4 * hno(band, h) + g
                    pool.wait_ge(s_fa, st + 1)
                    pool.wait_ge(s_fr, st + 1)
                    after(pool, s_os[g % 2], 16 * (2 * hno(band, h) + g // 2))
                    nc.gpsimd.tensor_tensor(f2[:], f2[:], f3[:], ALU.add).then_inc(s_fo, 1)
                    pool.wait_ge(s_fo, st + 1)
                    nc.gpsimd.tensor_tensor(fo[g % 2][:], f2[:], fr[:], ALU.mult).then_inc(s_fs, 1)
                    pool.wait_ge(s_fs, st + 1)

                def begin(band, h, u):
                    nc.gpsimd.memset(eye[:], 0.0).then_inc(s_eye, 1)
                    pool.wait_ge(s_eye, 1)
                    nc.gpsimd.affine_select(out=eye[:], in_=eye[:], compare_op=ALU.not_equal, fill=1.0, base=0,
                                            pattern=[[-1, P]], channel_multiplier=1).then_inc(s_eye, 1)
                    pool.wait_ge(s_eye, 2)
                    clear(band, h, u)
                    reduce(band, h, u, 0)

                def head(band, h, u, first, last):
                    nxt = following(band, h, last)
                    before = band and isinstance(h, int) and h == 0
                    for g in range(NG):
                        more = (band, h, u, g + 1) if g + 1 < NG else (*nxt, 1 - u, 0) if nxt else None
                        if g > 0:
                            finish(band, h, g - 1)
                        elif before:
                            finish(False, H - 1, NG - 1)
                        elif not first:
                            finish(band, h - 1, NG - 1)
                        if g == 1 and nxt:
                            clear(*nxt, 1 - u)
                        if more:
                            reduce(*more)
                    if nxt is None:
                        finish(band, h, NG - 1)

                walk(pool, begin, head)

            @block.vector
            def _(dve):
                def split_kv(band, h, u):
                    n = hno(band, h)
                    dve.wait_ge(s_ld, 16 * ND * (n + 1))
                    if n_pos(n):
                        dve.wait_ge(s_pv, prev_end(band, h))
                    nc.vector.tensor_copy(VA[u][:, :, 0:HD], vr[:]).then_inc(s_pd, 1)
                    nc.vector.tensor_copy(VB[u][:, :, 0:HD], vr[:])
                    nc.vector.tensor_copy(col[u][:, None, :], cols[:, ds(n, 1), :])
                    dve.wait_ge(s_pd, 5 * n + 1)
                    nc.vector.tensor_tensor(VA[u][:, :, HD:2 * HD], vr[:], f32(VA[u][:, :, 0:HD]), ALU.subtract).then_inc(s_pd, 1)
                    dve.wait_ge(s_pa, n + 1)
                    nc.vector.tensor_tensor(K2[u][0:64, :], kd[0:64, :], f32(K1[u][0:64, :]), ALU.subtract).then_inc(s_pd, 1)

                def split_q(band, h, u):
                    n = hno(band, h)
                    dve.wait_ge(s_pq, n + 1)
                    nc.vector.tensor_copy(Q2[u][0:64, :], f32(Q1[u][0:64, :])).then_inc(s_pd, 1)
                    nc.vector.scalar_tensor_tensor(Q1[u][64:128, :], qd[64:128, :], SCALE, f32(Q1[u][64:128, :]),
                                                   ALU.mult, ALU.subtract).then_inc(s_pd, 1)

                def maxima(band, h, u, g, j):
                    n = unit0(band, h) + start[band][g] + j
                    kt, c0, w, _ = U[band][g][j]
                    r = run[g % 2][:, c0:c0 + w]
                    if j == 0:
                        after(dve, s_ar, 4 * hno(band, h) + g - 1)
                    dve.wait_ge(s_mq, n + 1)
                    if j == 0:
                        nc.vector.tensor_scalar(r, sm[j % 2][:, :w], col[u][:, kt:kt + 1], None, ALU.add).then_inc(s_mx, 1)
                    else:
                        dve.wait_ge(s_mx, n)
                        nc.vector.scalar_tensor_tensor(r, sm[j % 2][:, :w], col[u][:, kt:kt + 1], r, ALU.add,
                                                       ALU.max).then_inc(s_mx, 1)

                def low(band, h, u, g, j):
                    n = unit0(band, h) + start[band][g] + j
                    w = U[band][g][j][2]
                    b = (start[band][g] + j) % NP
                    dve.wait_ge(s_hi, n + 1)
                    nc.vector.tensor_tensor(pl[b][:, :w], pr[b][:, :w], f32(ph[b][:, :w]), ALU.subtract).then_inc(s_lo, 1)

                def finish(band, h, g):
                    st = 4 * hno(band, h) + g
                    dve.wait_ge(s_fc, st + 1)
                    after(dve, s_fs, st)
                    nc.vector.reciprocal(fr[:], ob[g % 2][HD:P, :])
                    nc.vector.tensor_tensor(f3[:], oa[g % 2][0:HD, :], f1[:], ALU.add).then_inc(s_fa, 1)
                    nc.vector.drain().then_inc(s_fr, 1)

                def begin(band, h, u):
                    for v in range(2):
                        nc.vector.memset(K2[v][64:128, :].bitcast(F32), 0.0)
                    nc.vector.memset(VC[:, 0:HD].bitcast(F32), 0.0)
                    nc.vector.memset(VC[:, HD:2 * HD].bitcast(F32), 1.0)
                    for v in range(2):
                        nc.vector.memset(VB[v][:, :, HD:2 * HD].bitcast(F32), 1.0)
                    dve.drain()
                    for v in range(2):
                        nc.vector.memset(K2[v][64:65, :].bitcast(F32), 1.0)
                        nc.vector.memset(K2[v][96:97, :].bitcast(F32), 1.0)
                    dve.wait_ge(s_eye, 2)
                    nc.vector.tensor_copy(eyeR[:], eye[:])
                    nc.vector.drain().then_inc(s_cst, 1)
                    split_kv(band, h, u)
                    split_q(band, h, u)
                    for j in range(len(U[band][0])):
                        maxima(band, h, u, 0, j)
                    negate("dve", band, h, u, 0)

                def head(band, h, u, first, last):
                    nxt = following(band, h, last)
                    before = band and isinstance(h, int) and h == 0
                    for g in range(NG):
                        n_exp = len(U[band][g])
                        more = (band, h, u, g + 1) if g + 1 < NG else (*nxt, 1 - u, 0) if nxt else None
                        for kind, j in merged(n_exp, len(U[more[0]][more[3]]) if more else 0):
                            if kind == "M":
                                maxima(*more, j)
                                continue
                            if j == n_exp - 1 and more:
                                negate("dve", *more)
                            low(band, h, u, g, j)
                            if j == 2 and g > 0:
                                finish(band, h, g - 1)
                            elif j == 2 and before:
                                finish(False, H - 1, NG - 1)
                            elif j == 2 and not first:
                                finish(band, h - 1, NG - 1)
                            if g == 1 and nxt and j == 4:
                                split_kv(*nxt, 1 - u)
                            if g == 1 and nxt and j == 6:
                                split_q(*nxt, 1 - u)
                    if nxt is None:
                        finish(band, h, NG - 1)

                walk(dve, begin, head)


def attend_streams(nc, t):
    NKA, NKB = PAST_A // P, PAST_B // P
    LMAX = PAST_A + P
    EXT = PAST_B + 2 * NQ
    with ExitStack() as ctx:
        m = Mem(nc, ctx, "str")
        kr = [m.sb(f"kr{u}", [P, GW // P, LMAX]) for u in range(2)]
        vr = [m.sb(f"vr{u}", [P, NKA + 1, GW]) for u in range(2)]
        kh = m.sb("kh", [P, GW // P, LMAX], F32R)
        kl = m.sb("kl", [P, GW // P, LMAX], F32R)
        vh = m.sb("vh", [P, NKA + 1, GW], F32R)
        vl = m.sb("vl", [P, NKA + 1, GW], F32R)
        bt = [m.sb(f"bt{u}", [P, LMAX]) for u in range(2)]
        qr = m.sb("qr", [P, 2, GW // P, P])
        qh = m.sb("qh", [P, GW // P, P], F32R)
        ql = m.sb("ql", [P, GW // P, P], F32R)
        x = [m.sb(f"x{u}", [P, LMAX]) for u in range(2)]
        mx = m.sb("mx", [P, 4])
        nm = m.sb("nm", [P, 1])
        sums = [m.sb(f"sums{u}", [P, 1]) for u in range(2)]
        inv = m.sb("inv", [P, 1])
        pth = m.sb("pth", [P, NKA + 1, P], F32R)
        ptl = m.sb("ptl", [P, NKA + 1, P], F32R)
        om = m.sb("om", [P, GW])
        own = m.sb("own", [P, GW])
        mk = [m.sb(f"mk{v}", [P, P]) for v in range(2)]
        fold = m.sb("fold", [P, NQ])
        seen = m.sb("seen", [P, NQ])
        eye = m.sb("eye", [P, P])
        mo = m.sb("mo", [P, GW // P, P])
        rb = m.sb("rb", [H, 2 * CLIP + 1])
        ext = m.sb("ext", [H, EXT])
        ps = m.ps("ps", [P, 3, 512])
        pt = m.ps("pt", [P, 3, 512])
        po = m.ps("po", [P, 512])
        pm = m.ps("pm", [P, 512])
        lk = [m.sem(f"keys{u}") for u in range(2)]
        lv = [m.sem(f"values{u}") for u in range(2)]
        lb = [m.sem(f"bias{u}") for u in range(2)]
        (s_q, s_rb, s_ext, s_sk, s_c, s_z, s_kh, s_kl, s_bd, s_s, s_x, s_m, s_nm, s_e, s_vh, s_vl, s_t, s_ph, s_pl, s_o,
         s_iv, s_om, s_f, s_mo, s_st, s_k0) = (m.sem(n) for n in (
             "q", "rb", "ext", "skewed", "consts", "zeroed", "k_high", "k_low", "block_q", "scores", "biased", "maxed",
             "negmax", "exp", "v_high", "v_low", "turned", "p_high", "p_low", "pv", "inverse", "masked", "folded", "out",
             "stored", "cache"))
        CH = GW // P

        def walk(eng, begin, step, end):
            for band in range(2):
                begin(band)
                step(band, 1, 1)
                with eng.Fori(1, NB // 2) as i:
                    for u in range(2):
                        step(band, 2 * i + u, u)
                end(band)

        def nk(band):
            return NKB if band else NKA

        def pieces(band):
            L = nk(band) * P
            return [(i, c, min(512, L - c)) for i, c in enumerate(range(0, L, 512))] + [(L // 512, L, P)]

        with nc.Block() as block:

            @block.sync
            def _(sp):
                sp.dma_start(rb[:], t["rel_bias"]).then_inc(s_rb, 16)
                for band in range(2):
                    sp.dma_start(qr[:, band], t["zT"][band * 2 * GW:band * 2 * GW + GW, SEQ:].rearrange("(c p) t -> p c t", p=P))\
                        .then_inc(s_q, 16)
                sp.wait_ge(s_ext, 2)
                sp.dma_start(t["skew2"], ext[:, None, :].to_broadcast([H, NQ, EXT])).then_inc(s_sk, 16)
                sp.wait_ge(s_sk, 16)

                def load(band, b, u):
                    n = NB * band + b
                    L = nk(band) * P
                    after(sp, s_kl, n - 1)
                    keys, vals = (t["cache_bk"], t["cache_bv"]) if band else (t["cache_ak"], t["cache_av"])
                    k0 = band * 2 * GW + GW
                    sp.dma_start(kr[u][:, :, 0:L], keys[ds(b, 1)].rearrange("b p c s -> p (b c) s")).then_inc(lk[u], 16)
                    sp.dma_start(kr[u][:, :, L:L + NQ], t["zT"][k0:k0 + GW, ds(SEQ + b * NQ, NQ)].rearrange("(c p) t -> p c t", p=P))\
                        .then_inc(lk[u], 16)
                    after(sp, s_vl, n - 1)
                    sp.dma_start(vr[u][:, 0:nk(band), :], vals[ds(b, 1)].rearrange("b (a p) c -> p (b a) c", p=P)).then_inc(lv[u], 16)
                    sp.dma_start(vr[u][0:NQ, nk(band), :], t["v"][ds(SEQ + b * NQ, NQ), band * GW:(band + 1) * GW]).then_inc(lv[u], 16)
                    if band == 0:
                        after(sp, s_m, n - 1)
                        cs = t["csum"][ds(b * H, H), :]
                        sp.dma_start(bt[u][:, 0:L + NQ], cs[:, None, :].to_broadcast([H, NQ, L + NQ])).then_inc(lb[u], 16)

                def begin(band):
                    sp.wait_ge(s_z, band + 1)
                    if band:
                        sp.wait_ge(s_m, NB)
                        sk = t["skew2"]
                        for h in range(H):
                            sp.dma_start(bt[0][h * NQ:(h + 1) * NQ, 0:PAST_B + NQ],
                                         bass.AP(sk.tensor, sk.offset + h * NQ * EXT + NQ - 1,
                                                 [[EXT - 1, NQ], [1, PAST_B + NQ]])).then_inc(lb[0], 16)
                    load(band, 0, 0)

                walk(sp, begin, load, lambda band: None)
                for band in range(2):
                    sp.wait_ge(s_mo, band + 1)
                    sp.dma_start(t["mixT"][band * GW:(band + 1) * GW, SEQ:].rearrange("(c p) t -> p c t", p=P), mo[:])\
                        .then_inc(s_st, 16)
                    sp.wait_ge(s_st, 16 * (band + 1))

            @block.gpsimd
            def _(pool):
                c = [0]

                def step(ins):
                    c[0] += 1
                    ins.then_inc(s_c, 1)
                    pool.wait_ge(s_c, c[0])

                step(nc.gpsimd.memset(eye[:], 0.0))
                step(nc.gpsimd.affine_select(out=eye[:], in_=eye[:], compare_op=ALU.not_equal, fill=1.0, base=0,
                                             pattern=[[-1, P]], channel_multiplier=1))
                for tile in (mk[0], mk[1], fold):
                    step(nc.gpsimd.memset(tile[:], 0.0))
                step(nc.gpsimd.memset(own[:], 1.0))
                ov = own[:].rearrange("p (h d) -> p h d", h=H)
                step(nc.gpsimd.affine_select(out=ov, in_=ov, compare_op=ALU.is_ge, fill=0.0, base=0,
                                             pattern=[[-NQ, H], [0, HD]], channel_multiplier=1))
                step(nc.gpsimd.affine_select(out=ov, in_=ov, compare_op=ALU.is_ge, fill=0.0, base=NQ - 1,
                                             pattern=[[NQ, H], [0, HD]], channel_multiplier=-1))
                for h in range(H):
                    step(nc.gpsimd.affine_select(out=fold[:], in_=fold[:], compare_op=ALU.not_equal, fill=1.0, base=-NQ * h,
                                                 pattern=[[-1, NQ]], channel_multiplier=1))
                for v in range(2):
                    step(nc.gpsimd.memset(mk[v][:, NQ:], NEG))

            @block.tensor
            def _(pe):
                pe.wait_ge(s_c, 18)

                def score(band, b):
                    n = NB * band + b
                    pe.wait_ge(s_kl, n + 1)
                    pe.wait_ge(s_bd, n + 1)
                    after(pe, s_m, n)
                    for bank, c0, w in pieces(band):
                        last = three(nc, ps[:, bank, :w], CH, lambda k: qh[:, k, :], lambda k: ql[:, k, :],
                                     lambda k: kh[:, k, c0:c0 + w], lambda k: kl[:, k, c0:c0 + w])
                    last.then_inc(s_s, 1)

                def value(band, b, u):
                    n = NB * band + b
                    pe.wait_ge(s_e, n + 1)
                    after(pe, s_pl, n)
                    for a in range(nk(band) + 1):
                        last = nc.tensor.transpose(pt[:, a // 4, a % 4 * P:(a % 4 + 1) * P], x[u][:, a * P:(a + 1) * P], eye[:])
                    last.then_inc(s_t, 1)
                    pe.wait_ge(s_pl, n + 1)
                    pe.wait_ge(s_vl, n + 1)
                    after(pe, s_om, n)
                    three(nc, po[:], nk(band) + 1, lambda k: pth[:, k, :], lambda k: ptl[:, k, :],
                          lambda k: vh[:, k, :], lambda k: vl[:, k, :]).then_inc(s_o, 1)
                    pe.wait_ge(s_om, n + 1)
                    if band and isinstance(b, int) and b == 0:
                        pe.wait_ge(s_mo, 1)
                    for k in range(CH):
                        last = nc.tensor.matmul(pm[:].rearrange("p (c t) -> p c t", c=CH)[:, k, ds(b * NQ, NQ)],
                                                om[:, k * P:(k + 1) * P], fold[:], start=True, stop=True)
                    last.then_inc(s_f, 1)

                def step(band, b, u):
                    score(band, b)
                    value(band, b - 1, 1 - u)

                walk(pe, lambda band: score(band, 0), step, lambda band: value(band, NB - 1, 1))

            @block.scalar
            def _(act):
                def keys(band, b, u):
                    n = NB * band + b
                    L = (nk(band) + 1) * P
                    act.wait_ge(lk[u], 32 * (band * NB // 2) + 16 * (b - u) + 32)
                    after(act, s_s, n)
                    nc.scalar.activation(kh[:, :, :L], kr[u][:, :, :L], ACT.Copy).then_inc(s_kh, 1)

                def values(band, b, u):
                    n = NB * band + b
                    act.wait_ge(lv[u], 32 * (band * NB // 2) + 16 * (b - u) + 32)
                    after(act, s_o, n)
                    nc.scalar.activation(vh[:, :nk(band) + 1, :], vr[u][:, :nk(band) + 1, :], ACT.Copy).then_inc(s_vh, 1)

                def exps(band, b, u):
                    n = NB * band + b
                    act.wait_ge(s_nm, n + 1)
                    L = (nk(band) + 1) * P
                    nc.scalar.activation(x[u][:, :L], x[u][:, :L], ACT.Exp, bias=nm[:, 0:1], accum_out=sums[u][:]).then_inc(s_e, 1)

                def turned(band, b):
                    n = NB * band + b
                    act.wait_ge(s_t, n + 1)
                    after(act, s_o, n)
                    k = nk(band) + 1
                    nc.scalar.activation(pth[:, :k, :].rearrange("p a t -> p (a t)"),
                                         pt[:].rearrange("p b t -> p (b t)")[:, :k * P], ACT.Copy).then_inc(s_ph, 1)

                def begin(band):
                    keys(band, 0, 0)
                    exps(band, 0, 0)
                    keys(band, 1, 1)

                def step(band, b, u, more=True):
                    values(band, b - 1, 1 - u)
                    exps(band, b, u)
                    turned(band, b - 1)
                    if more:
                        keys(band, b + 1, 1 - u)

                def end(band):
                    values(band, NB - 1, 1)
                    turned(band, NB - 1)

                for band in range(2):
                    begin(band)
                    step(band, 1, 1)
                    with act.Fori(1, NB // 2 - 1) as i:
                        for u in range(2):
                            step(band, 2 * i + u, u)
                    step(band, NB - 2, 0)
                    step(band, NB - 1, 1, more=False)
                    end(band)

            @block.vector
            def _(dve):
                dve.wait_ge(s_rb, 16)
                near = PAST_B + NQ - 1 - CLIP
                nc.vector.tensor_scalar(ext[:, 0:near], rb[:, 2 * CLIP:].to_broadcast([H, near]), -1.0, None, ALU.mult).then_inc(s_ext, 1)
                nc.vector.tensor_scalar(ext[:, near:], rb[:, 2 * CLIP - (EXT - 1 - near):][:, ::-1], -1.0, None, ALU.mult).then_inc(s_ext, 1)
                nc.vector.memset(qh[:].bitcast(F32), 0.0)
                nc.vector.memset(ql[:].bitcast(F32), 0.0)
                dve.drain()
                dve.wait_ge(s_c, 18)
                nc.vector.tensor_tensor_scan(seen[:], fold[:], fold[:], 0.0, ALU.add, ALU.bypass).then_inc(s_ext, 1)
                dve.wait_ge(s_ext, 3)
                nc.vector.tensor_scalar(mk[0][:, 1:NQ], seen[:, 0:NQ - 1], NEG, None, ALU.mult)
                dve.drain()
                dve.wait_ge(s_q, 32)

                def block_q(band, b):
                    n = NB * band + b
                    after(dve, s_s, n)
                    for r in range(2):
                        rows = slice(64 * r, 64 * r + 64)
                        src = qr[rows, band, :, ds(b * NQ, NQ)]
                        h = qh[rows, 0, r * NQ:(r + 1) * NQ]
                        l = ql[rows, 0, r * NQ:(r + 1) * NQ]
                        hv, lv_ = (bass.AP(a.tensor, a.offset, [a.ap[0], [P + 2 * NQ, CH], [1, NQ]]) for a in (h, l))
                        nc.vector.tensor_scalar(hv, src, SCALE, None, ALU.mult).then_inc(s_k0, 1)
                        dve.wait_ge(s_k0, 2 * n + r + 1)
                        last = nc.vector.scalar_tensor_tensor(lv_, src, SCALE, hv.bitcast(F32), ALU.mult, ALU.subtract)
                    last.then_inc(s_bd, 1)

                def keys(band, b, u):
                    n = NB * band + b
                    L = (nk(band) + 1) * P
                    dve.wait_ge(s_kh, n + 1)
                    nc.vector.tensor_tensor(kl[:, :, :L], kr[u][:, :, :L], f32(kh[:, :, :L]), ALU.subtract).then_inc(s_kl, 1)
                    block_q(band, b)

                def values(band, b, u):
                    n = NB * band + b
                    k = nk(band) + 1
                    dve.wait_ge(s_vh, n + 1)
                    nc.vector.tensor_tensor(vl[:, :k, :], vr[u][:, :k, :], f32(vh[:, :k, :]), ALU.subtract).then_inc(s_vl, 1)

                def maxima(band, b, u):
                    n = NB * band + b
                    bias = bt[0] if band else bt[u]
                    if band:
                        dve.wait_ge(lb[0], 16 * (NB // 2 + H))
                    else:
                        dve.wait_ge(lb[u], 8 * (b - u) + 16)
                    dve.wait_ge(s_s, n + 1)
                    after(dve, s_t, n - 1)
                    after(dve, s_e, n)
                    pcs = pieces(band)
                    for bank, c0, w in pcs:
                        nc.vector.tensor_tensor(x[u][:, c0:c0 + w], ps[:, bank, :w], bias[:, c0:c0 + w], ALU.subtract).then_inc(s_x, 1)
                    L = pcs[-1][1]
                    done = 4 * n if not band else 4 * NB + 3 * (n - NB)
                    dve.wait_ge(s_x, done + len(pcs))
                    nc.vector.tensor_tensor(x[u][:, L:L + P], x[u][:, L:L + P], mk[band][:], ALU.add).then_inc(s_x, 1)
                    dve.wait_ge(s_x, done + len(pcs) + 1)
                    nc.vector.reduce_max(mx[:, 0:1], x[u][:, 0:L + P], AX.X).then_inc(s_m, 1)
                    dve.wait_ge(s_m, n + 1)
                    nc.vector.tensor_scalar(nm[:], mx[:, 0:1], -1.0, None, ALU.mult).then_inc(s_nm, 1)

                def turned(band, b):
                    n = NB * band + b
                    k = nk(band) + 1
                    dve.wait_ge(s_ph, n + 1)
                    nc.vector.tensor_tensor(ptl[:, :k, :].rearrange("p a t -> p (a t)"),
                                            pt[:].rearrange("p b t -> p (b t)")[:, :k * P],
                                            f32(pth[:, :k, :]).rearrange("p a t -> p (a t)"), ALU.subtract).then_inc(s_pl, 1)

                def outputs(band, b, u):
                    n = NB * band + b
                    dve.wait_ge(s_e, n + 1)
                    after(dve, s_om, n)
                    nc.vector.reciprocal(inv[:], sums[u][:]).then_inc(s_iv, 1)
                    dve.wait_ge(s_iv, n + 1)
                    dve.wait_ge(s_o, n + 1)
                    after(dve, s_f, n)
                    nc.vector.scalar_tensor_tensor(om[:], po[:], inv[:, 0:1], own[:], ALU.mult, ALU.mult).then_inc(s_om, 1)

                def begin(band):
                    for u in range(2):
                        L = nk(band) * P
                        nc.vector.memset(kr[u][:, :, L:L + P], 0.0)
                        nc.vector.memset(vr[u][:, nk(band), :], 0.0)
                        nc.vector.memset(bt[u][:, L:L + P], 0.0)
                    dve.drain().then_inc(s_z, 1)
                    keys(band, 0, 0)
                    maxima(band, 0, 0)
                    keys(band, 1, 1)

                def step(band, b, u, more=True):
                    values(band, b - 1, 1 - u)
                    maxima(band, b, u)
                    turned(band, b - 1)
                    outputs(band, b - 1, 1 - u)
                    if more:
                        keys(band, b + 1, 1 - u)

                for band in range(2):
                    begin(band)
                    step(band, 1, 1)
                    with dve.Fori(1, NB // 2 - 1) as i:
                        for u in range(2):
                            step(band, 2 * i + u, u)
                    step(band, NB - 2, 0)
                    step(band, NB - 1, 1, more=False)
                    values(band, NB - 1, 1)
                    turned(band, NB - 1)
                    outputs(band, NB - 1, 1)
                    dve.wait_ge(s_f, NB * (band + 1))
                    if band:
                        dve.wait_ge(s_st, 16)
                    nc.vector.tensor_copy(mo[:].rearrange("p c t -> p (c t)"), pm[:]).then_inc(s_mo, 1)


def mix_out(nc, t):
    HALF = 512
    with ExitStack() as ctx:
        m = Mem(nc, ctx, "mix")
        wr = m.sb("wr", [P, D])
        wh = m.sb("wh", [P, KD, D], F32R)
        wl = m.sb("wl", [P, KD, D], F32R)
        g_mix = m.sb("g_mix", [P, KD])
        g_ffn = m.sb("g_ffn", [P, KD])
        g_post = m.sb("g_post", [P, D])
        ones = m.sb("ones", [P, P])
        eye = m.sb("eye", [P, P])
        power = m.sb("power", [P, 2])
        o = [m.sb(f"o{u}", [P, KD, P]) for u in range(2)]
        xr = [m.sb(f"xr{u}", [P, D]) for u in range(2)]
        sq = m.sb("sq", [P, KD, P])
        ss = m.sb("ss", [P, 2, P])
        var = m.sb("var", [P, 2])
        r = m.sb("r", [P, 2])
        dg = m.sb("dg", [P, 2, P])
        oh = [m.sb(f"oh{u}", [P, KD, P], F32R) for u in range(2)]
        ol = [m.sb(f"ol{u}", [P, KD, P], F32R) for u in range(2)]
        junk = m.sb("junk", [P, D])
        s1 = m.sb("s1", [P, 1])
        v1 = m.sb("v1", [P, 1])
        r1 = m.sb("r1", [P, 1])
        s2 = m.sb("s2", [P, 1])
        v2 = m.sb("v2", [P, 1])
        r2 = m.sb("r2", [P, 1])
        y = m.sb("y", [P, D])
        x1 = [m.sb(f"x1{u}", [P, D]) for u in range(2)]
        h = m.sb("h", [P, D])
        ht = [m.sb(f"ht{u}", [P, KD, P]) for u in range(2)]
        pn = m.ps("pn", [P, 512])
        py = [m.ps(f"py{u}", [P, D]) for u in range(2)]
        pt = m.ps("pt", [P, D])
        lo_ = [m.sem(f"in{u}") for u in range(2)]
        lx = [m.sem(f"x{u}") for u in range(2)]
        st1 = [m.sem(f"x1_stored{u}") for u in range(2)]
        sth = [m.sem(f"h_stored{u}") for u in range(2)]
        (s_g, s_w, s_wh, s_wl, s_c, s_cv, s_sq, s_ss, s_pn, s_var, s_r, s_on, s_oh, s_ol, s_y, s_s1, s_v1, s_r1, s_y1, s_x1,
         s_s2, s_v2, s_r2, s_h, s_t, s_ht, s_carry, s_dg, s_pr) = (m.sem(n) for n in (
             "gains", "w", "w_high", "w_low", "consts", "consts_v", "squares", "summed", "totals", "var", "rms", "normed", "high",
             "low", "products", "sum1", "var1", "rms1", "post", "resid", "sum2", "var2", "rms2", "h", "turned", "h_out",
             "carry", "diagonal", "spread"))

        def walk(eng, it):
            for t_ in (-1, 0, 1):
                it(t_, t_ % 2)
            with eng.Fori(0, (NT - 3) // 2) as i:
                for u in range(2):
                    it(2 * i + 2 + u, u)
            for t_ in (NT - 1, NT, NT + 1):
                it(t_, t_ % 2)

        def real(t_):
            return not isinstance(t_, int) or 0 <= t_ < NT

        def rounds(t_, u):
            return (t_ - u) * 8 + 16

        m.clear_sems()
        with nc.Block() as block:

            @block.sync
            def _(sp):
                sp.dma_start(g_mix[:], t["g_mix"]).then_inc(s_g, 16)
                sp.dma_start(g_ffn[:], t["g_ffn"]).then_inc(s_g, 16)
                sp.dma_start(g_post[:], t["g_post"].to_broadcast([P, D])).then_inc(s_g, 16)
                for k in range(KD):
                    after(sp, s_wl, k)
                    sp.dma_start(wr[:], t["w_out"][k]).then_inc(s_w, 16)

                def load(t_, u):
                    after(sp, s_ol, t_ - 1)
                    sp.dma_start(o[u][:], t["mixT"].rearrange("(k p) t -> p k t", p=P)[:, :, ds(t_ * P, P)]).then_inc(lo_[u], 16)
                    after(sp, s_x1, t_ - 1)
                    sp.dma_start(xr[u][:], t["x"][ds(t_ * P, P), :]).then_inc(lx[u], 16)

                def it(t_, u):
                    if real(t_ + 1):
                        load(t_ + 1, 1 - u)
                    if real(t_ - 1):
                        sp.wait_ge(s_x1, t_)
                        sp.dma_start(t["x1"][ds((t_ - 1) * P, P), :], x1[1 - u][:]).then_inc(st1[1 - u], 16)
                    if real(t_ - 2):
                        sp.wait_ge(s_ht, t_ - 1)
                        sp.sem_inc(s_carry, 1)
                        sp.dma_start(t["hT"][:, :, ds((t_ - 2) * P, P)], ht[u][:]).then_inc(sth[u], 16)

                walk(sp, it)
                for u in range(2):
                    sp.wait_ge(st1[u], 16 * ((NT + 1 - u) // 2))
                    sp.wait_ge(sth[u], 16 * ((NT + 1 - u) // 2))

            @block.scalar
            def _(act):
                for k in range(KD):
                    act.wait_ge(s_w, 16 * (k + 1))
                    nc.scalar.activation(wr[:], wr[:], ACT.Copy, scale=g_mix[:, k:k + 1]).then_inc(s_wh, 1)
                    act.wait_ge(s_wh, 2 * k + 1)
                    nc.scalar.activation(wh[:, k, :], wr[:], ACT.Copy).then_inc(s_wh, 1)

                def it(t_, u):
                    v = 1 - u
                    if real(t_ + 1):
                        act.wait_ge(lo_[v], rounds(t_ + 1, v))
                        after(act, s_ss, t_ + 1)
                        nc.scalar.activation(sq[:], o[v][:], ACT.Square).then_inc(s_sq, 1)
                        act.wait_ge(s_on, t_ + 2)
                        after(act, s_y, t_)
                        nc.scalar.activation(oh[v][:], o[v][:], ACT.Copy).then_inc(s_oh, 1)
                    if real(t_ - 1):
                        act.wait_ge(s_y, t_)
                        nc.scalar.activation(junk[:], py[v][:], ACT.Square, accum_out=s1[:]).then_inc(s_s1, 1)
                        act.wait_ge(s_x1, t_)
                        act.wait_ge(s_s1, t_)
                        nc.scalar.activation(junk[:], x1[v][:], ACT.Square, accum_out=s2[:]).then_inc(s_s2, 1)
                        act.wait_ge(s_r2, t_)
                        after(act, s_t, t_ - 1)
                        nc.scalar.activation(h[:], x1[v][:], ACT.Copy, scale=r2[:, 0:1]).then_inc(s_h, 1)

                walk(act, it)

            @block.gpsimd
            def _(pool):
                nc.gpsimd.memset(eye[:], 0.0).then_inc(s_c, 1)
                pool.wait_ge(s_c, 1)
                nc.gpsimd.affine_select(out=eye[:], in_=eye[:], compare_op=ALU.not_equal, fill=1.0, base=0,
                                        pattern=[[-1, P]], channel_multiplier=1).then_inc(s_c, 1)
                pool.wait_ge(s_c, 2)
                nc.gpsimd.memset(power[:], -0.5).then_inc(s_c, 1)
                pool.wait_ge(s_c, 3)

                def it(t_, u):
                    v = 1 - u
                    if real(t_ + 1):
                        pool.wait_ge(s_var, t_ + 2)
                        after(pool, s_dg, t_ + 1)
                        nc.gpsimd.tensor_tensor(r[:], var[:], power[:], ALU.pow).then_inc(s_r, 1)
                    if real(t_ - 1):
                        pool.wait_ge(s_v1, t_)
                        after(pool, s_y1, t_ - 1)
                        nc.gpsimd.tensor_tensor(r1[:], v1[:], power[:, 0:1], ALU.pow).then_inc(s_r1, 1)
                        pool.wait_ge(s_y1, t_)
                        pool.wait_ge(lx[v], rounds(t_ - 1, v))
                        after(pool, st1[v], rounds(t_ - 1, v) - 16)
                        after(pool, s_h, t_ - 2)
                        nc.gpsimd.tensor_tensor(x1[v][:], y[:], xr[v][:], ALU.add).then_inc(s_x1, 1)
                        pool.wait_ge(s_v2, t_)
                        after(pool, s_h, t_ - 1)
                        nc.gpsimd.tensor_tensor(r2[:], v2[:], power[:, 0:1], ALU.pow).then_inc(s_r2, 1)

                walk(pool, it)

            @block.tensor
            def _(pe):
                pe.wait_ge(s_wl, KD)
                pe.wait_ge(s_c, 3)
                pe.wait_ge(s_cv, 1)

                def it(t_, u):
                    v = 1 - u
                    if real(t_ + 1):
                        pe.wait_ge(s_ss, t_ + 2)
                        after(pe, s_on, t_ + 1)
                        for g in range(2):
                            last = nc.tensor.matmul(pn[:, 2 * P + g:2 * P + g + 1], ss[:, g, :], ones[:, 0:1], start=True, stop=True)
                        last.then_inc(s_pn, 1)

                    def spread():
                        if real(t_ + 1):
                            pe.wait_ge(s_dg, t_ + 2)
                            nc.tensor.matmul(pn[:, 0:2 * P], ones[:], dg[:].rearrange("p g t -> p (g t)"), start=True, stop=True)\
                                .then_inc(s_pr, 1)

                    if real(t_):
                        pe.wait_ge(s_ol, t_ + 1)
                        after(pe, s_y1, t_ - 1)
                        after(pe, s_s1, t_ - 1)
                        for c in range(2):
                            cs = slice(c * HALF, (c + 1) * HALF)
                            last = three(nc, py[u][:, cs], KD, lambda k: oh[u][:, k, :], lambda k: ol[u][:, k, :],
                                         lambda k: wh[:, k, cs], lambda k: wl[:, k, cs])
                            if c == 1:
                                last.then_inc(s_y, 1)
                            else:
                                spread()
                    else:
                        spread()
                    if real(t_ - 1):
                        pe.wait_ge(s_h, t_)
                        after(pe, s_ht, t_ - 1)
                        for k in range(KD):
                            last = nc.tensor.transpose(pt[:, k * P:(k + 1) * P], h[:, k * P:(k + 1) * P], eye[:])
                        last.then_inc(s_t, 1)

                walk(pe, it)

            @block.vector
            def _(dve):
                nc.vector.memset(ones[:], 1.0).then_inc(s_cv, 1)
                dve.wait_ge(s_c, 2)
                dve.wait_ge(s_g, 48)
                for k in range(KD):
                    dve.wait_ge(s_wh, 2 * k + 2)
                    nc.vector.tensor_tensor(wl[:, k, :], wr[:], f32(wh[:, k, :]), ALU.subtract).then_inc(s_wl, 1)

                def it(t_, u):
                    v = 1 - u
                    if real(t_ - 2):
                        dve.wait_ge(s_t, t_ - 1)
                        after(dve, sth[u], rounds(t_ - 2, u) - 16)
                        for c in range(2):
                            last = nc.vector.tensor_tensor(ht[u][:, 4 * c:4 * c + 4, :],
                                                           pt[:, c * HALF:(c + 1) * HALF].rearrange("p (k t) -> p k t", k=4),
                                                           g_ffn[:, 4 * c:4 * c + 4, None].to_broadcast([P, 4, P]), ALU.mult)
                        last.then_inc(s_ht, 1)
                    if real(t_ + 1):
                        dve.wait_ge(s_sq, t_ + 2)
                        after(dve, s_pn, t_ + 1)
                        nc.vector.tensor_reduce(ss[:], sq[:].rearrange("p (g c) t -> p g t c", g=2), AX.X, ALU.add).then_inc(s_ss, 1)
                        dve.wait_ge(s_pn, t_ + 2)
                        after(dve, s_r, t_ + 1)
                        nc.vector.tensor_scalar(var[:], pn[:, 2 * P:2 * P + 2], 1.0 / GW, EPS, ALU.mult, ALU.add).then_inc(s_var, 1)
                        dve.wait_ge(s_r, t_ + 2)
                        after(dve, s_pr, t_ + 1)
                        for g in range(2):
                            last = nc.vector.tensor_scalar(dg[:, g, :], eye[:], r[:, g:g + 1], None, ALU.mult)
                        last.then_inc(s_dg, 1)
                        dve.wait_ge(s_pr, t_ + 2)
                        nc.vector.tensor_tensor(o[v][:].rearrange("p (g c) t -> p g c t", g=2), o[v][:].rearrange("p (g c) t -> p g c t", g=2),
                                                pn[:, 0:2 * P].rearrange("p (g t) -> p g t", g=2)[:, :, None, :]
                                                .to_broadcast([P, 2, KD // 2, P]), ALU.mult).then_inc(s_on, 1)
                        dve.wait_ge(s_oh, t_ + 2)
                        nc.vector.tensor_tensor(ol[v][:], o[v][:], f32(oh[v][:]), ALU.subtract).then_inc(s_ol, 1)
                    if real(t_ - 1):
                        dve.wait_ge(s_s1, t_)
                        after(dve, s_r1, t_ - 1)
                        nc.vector.tensor_scalar(v1[:], s1[:], 1.0 / D, EPS, ALU.mult, ALU.add).then_inc(s_v1, 1)
                        dve.wait_ge(s_r1, t_)
                        after(dve, s_x1, t_ - 1)
                        nc.vector.scalar_tensor_tensor(y[:], py[v][:], r1[:, 0:1], g_post[:], ALU.mult, ALU.mult).then_inc(s_y1, 1)
                        dve.wait_ge(s_s2, t_)
                        after(dve, s_r2, t_ - 1)
                        nc.vector.tensor_scalar(v2[:], s2[:], 1.0 / D, EPS, ALU.mult, ALU.add).then_inc(s_v2, 1)

                walk(dve, it)


def feed_forward(nc, t):
    NBL = (NT + 2) // 3
    TM = 3 * P
    assert NJ % 2 == 0 and NT % 3 == 2
    with ExitStack() as ctx:
        m = Mem(nc, ctx, "ffn")
        wgr = [m.sb(f"wgr{u}", [P, 2, KD, P]) for u in range(2)]
        wgh = [m.sb(f"wgh{u}", [P, 2, KD, P], F32R) for u in range(2)]
        wgl = [m.sb(f"wgl{u}", [P, 2, KD, P], F32R) for u in range(2)]
        wdr = [m.sb(f"wdr{u}", [P, D]) for u in range(2)]
        wdh = [m.sb(f"wdh{u}", [P, D], F32R) for u in range(2)]
        wdl = [m.sb(f"wdl{u}", [P, D], F32R) for u in range(2)]
        hr = m.sb("hr", [P, KD, TM])
        hh = m.sb("hh", [P, KD, TM], F32R)
        hl = m.sb("hl", [P, KD, TM], F32R)
        sg = m.sb("sg", [P, TM])
        a = m.sb("a", [P, TM])
        ah = [m.sb(f"ah{u}", [P, TM], F32R) for u in range(2)]
        al = [m.sb(f"al{u}", [P, TM], F32R) for u in range(2)]
        ys = m.sb("ys", [P, 3, D])
        x1 = m.sb("x1", [P, 3, D])
        g_post = m.sb("g_post", [P, D])
        power = m.sb("power", [P, 4])
        junk = m.sb("junk", [P, D])
        ss = m.sb("ss", [P, 3])
        vv = m.sb("vv", [P, 3])
        rr = m.sb("rr", [P, 3])
        pg = m.ps("pg", [P, 512])
        pu = m.ps("pu", [P, 512])
        py = m.ps("py", [P, 3, D])
        lw = [m.sem(f"wg{u}") for u in range(2)]
        ld = [m.sem(f"wd{u}") for u in range(2)]
        (s_g, s_pw, s_h, s_x1, s_gh, s_gl, s_dh, s_dl, s_hh, s_hl, s_pg, s_pu, s_sg, s_a, s_ah, s_al, s_dn, s_ye, s_yv, s_ss,
         s_vv, s_rr, s_y1, s_y2, s_st) = (m.sem(n) for n in (
             "gain", "power", "h", "x1", "wg_high", "wg_low", "wd_high", "wd_low", "h_high", "h_low", "gate", "up", "silu", "act",
             "act_high", "act_low", "down", "y_out_s", "y_out_v", "ss", "var", "rms", "post", "resid", "stored"))

        def walk(eng, first, step, last):
            def blk(b, nt):
                first(b, nt)
                step(b, nt, 0, 0)
                with eng.Fori(0, NJ // 2 - 1) as i:
                    for u in (1, 0):
                        step(b, nt, 2 * i + 2 - u, u)
                step(b, nt, NJ - 1, 1)
                last(b, nt)
            blk(0, 3)
            with eng.Fori(1, NBL - 1) as b:
                blk(b, 3)
            blk(NBL - 1, 2)

        m.clear_sems()
        with nc.Block() as block:

            @block.sync
            def _(sp):
                sp.dma_start(g_post[:], t["g_fpost"].to_broadcast([P, D])).then_inc(s_g, 16)

                def first(b, nt):
                    after(sp, s_hl, b)
                    sp.dma_start(hr[:, :, :nt * P], t["hT"][:, :, ds(b * TM, nt * P)]).then_inc(s_h, 16)

                def step(b, nt, j, u):
                    n = b * NJ + j
                    after(sp, s_gl, n - 1)
                    sp.dma_start(wgr[u][:], t["w_gu"][ds(j, 1)].rearrange("j p a k c -> p (j a) k c")).then_inc(lw[u], 16)
                    after(sp, s_dl, n - 1)
                    sp.dma_start(wdr[u][:], t["w_dn"][ds(j, 1)].rearrange("j p c -> p (j c)")).then_inc(ld[u], 16)
                    if isinstance(j, int) and j == NJ - 1:
                        if not isinstance(b, int) or b > 0:
                            store(b - 1, 3)
                            sp.wait_ge(s_st, 16 * b)
                        sp.dma_start(x1[:, :nt, :], t["x1"].rearrange("(n p) c -> p n c", p=P)[:, ds(b * 3, nt), :]).then_inc(s_x1, 16)

                def store(b, nt):
                    sp.wait_ge(s_y2, 3 * b + nt)
                    sp.dma_start(t["y"].rearrange("(n p) c -> p n c", p=P)[:, ds(b * 3, nt), :], x1[:, :nt, :]).then_inc(s_st, 16)

                walk(sp, first, step, lambda b, nt: None)
                store(NBL - 1, 2)
                sp.wait_ge(s_st, 16 * NBL)

            @block.tensor
            def _(pe):
                def first(b, nt):
                    pe.wait_ge(s_hl, b + 1)

                def step(b, nt, j, u):
                    n = b * NJ + j
                    w = nt * P
                    pe.wait_ge(s_gl, n + 1)
                    after(pe, s_sg, n)
                    three(nc, pg[:, :w], KD, lambda k: wgh[u][:, 0, k, :], lambda k: wgl[u][:, 0, k, :],
                          lambda k: hh[:, k, :w], lambda k: hl[:, k, :w]).then_inc(s_pg, 1)
                    after(pe, s_a, n)
                    three(nc, pu[:, :w], KD, lambda k: wgh[u][:, 1, k, :], lambda k: wgl[u][:, 1, k, :],
                          lambda k: hh[:, k, :w], lambda k: hl[:, k, :w]).then_inc(s_pu, 1)
                    if not (isinstance(j, int) and j == 0):
                        down(b, nt, j - 1, 1 - u)

                def down(b, nt, j, u):
                    n = b * NJ + j
                    pe.wait_ge(s_dl, n + 1)
                    pe.wait_ge(s_al, n + 1)
                    head = j == 0 if isinstance(j, int) else False
                    if head:
                        after(pe, s_ye, b)
                        after(pe, s_yv, b)
                    tail = isinstance(j, int) and j == NJ - 1
                    for q in range(nt):
                        for c in range(2):
                            out = py[:, q, c * 512:(c + 1) * 512]
                            cs = slice(c * 512, (c + 1) * 512)
                            qs = slice(q * P, (q + 1) * P)
                            nc.tensor.matmul(out, ah[u][:, qs], wdh[u][:, cs], start=head, stop=False, skip_group_check=True)
                            nc.tensor.matmul(out, ah[u][:, qs], wdl[u][:, cs], start=False, stop=False, skip_group_check=True)
                            last = nc.tensor.matmul(out, al[u][:, qs], wdh[u][:, cs], start=False, stop=tail, skip_group_check=True)
                    last.then_inc(s_dn, 1)

                def last(b, nt):
                    down(b, nt, NJ - 1, 1)

                def blk(b, nt):
                    first(b, nt)
                    step(b, nt, 0, 0)
                    step(b, nt, 1, 1)
                    with pe.Fori(1, NJ // 2 - 1) as i:
                        for u in range(2):
                            step(b, nt, 2 * i + u, u)
                    step(b, nt, NJ - 2, 0)
                    step(b, nt, NJ - 1, 1)
                    last(b, nt)

                blk(0, 3)
                with pe.Fori(1, NBL - 1) as b:
                    blk(b, 3)
                blk(NBL - 1, 2)

            def round_of(b, j, u):
                return (b * NJ + j - u) * 8 + 16

            @block.scalar
            def _(act):
                def split_gate(b, j, u):
                    n = b * NJ + j
                    act.wait_ge(lw[u], round_of(b, j, u))
                    after(act, s_pu, n - 1)
                    nc.scalar.activation(wgh[u][:], wgr[u][:], ACT.Copy).then_inc(s_gh, 1)

                def split_down(b, j, u):
                    n = b * NJ + j
                    act.wait_ge(ld[u], round_of(b, j, u))
                    after(act, s_dn, n - 1)
                    nc.scalar.activation(wdh[u][:], wdr[u][:], ACT.Copy).then_inc(s_dh, 1)

                def first(b, nt):
                    act.wait_ge(s_h, 16 * b + 16)
                    after(act, s_pu, NJ * b)
                    nc.scalar.activation(hh[:, :, :nt * P], hr[:, :, :nt * P], ACT.Copy).then_inc(s_hh, 1)

                def step(b, nt, j, u):
                    n = b * NJ + j
                    more = not (isinstance(j, int) and j + 1 == NJ and isinstance(b, int) and b == NBL - 1)
                    if more:
                        split_gate(b, j + 1, 1 - u)
                    act.wait_ge(s_pg, n + 1)
                    after(act, s_a, n)
                    nc.scalar.activation(sg[:, :nt * P], pg[:, :nt * P], ACT.Silu).then_inc(s_sg, 1)
                    if more:
                        split_down(b, j + 1, 1 - u)

                def last(b, nt):
                    act.wait_ge(s_dn, NJ * (b + 1))
                    after(act, s_y2, 3 * b)
                    for q in range(nt):
                        if q == 0:
                            nc.scalar.activation(ys[:, q, :], py[:, q, :], ACT.Copy)
                        if q == 1:
                            nc.scalar.activation(ys[:, q, 0:512], py[:, q, 0:512], ACT.Copy)
                    act.drain().then_inc(s_ye, 1)
                    act.wait_ge(s_yv, b + 1)
                    act.wait_ge(s_ye, b + 1)
                    for q in range(nt):
                        nc.scalar.activation(junk[:], ys[:, q, :], ACT.Square, accum_out=ss[:, q:q + 1]).then_inc(s_ss, 1)
                        act.wait_ge(s_ss, 3 * b + q + 1)

                split_gate(0, 0, 0)
                split_down(0, 0, 0)
                walk(act, first, step, last)

            @block.gpsimd
            def _(pool):
                nc.gpsimd.memset(power[:], -0.5).then_inc(s_pw, 1)
                pool.wait_ge(s_pw, 1)

                def last(b, nt):
                    pool.wait_ge(s_vv, b + 1)
                    nc.gpsimd.tensor_tensor(rr[:, :nt], vv[:, :nt], power[:, :nt], ALU.pow).then_inc(s_rr, 1)
                    pool.wait_ge(s_x1, 16 * b + 16)
                    for q in range(nt):
                        pool.wait_ge(s_y1, 3 * b + q + 1)
                        nc.gpsimd.tensor_tensor(x1[:, q, :], x1[:, q, :], ys[:, q, :], ALU.add).then_inc(s_y2, 1)

                last(0, 3)
                with pool.Fori(1, NBL - 1) as b:
                    last(b, 3)
                last(NBL - 1, 2)

            @block.vector
            def _(dve):
                dve.wait_ge(s_g, 16)

                def split_gate(b, j, u):
                    n = b * NJ + j
                    dve.wait_ge(s_gh, n + 1)
                    nc.vector.tensor_tensor(wgl[u][:], wgr[u][:], f32(wgh[u][:]), ALU.subtract).then_inc(s_gl, 1)

                def split_down(b, j, u):
                    n = b * NJ + j
                    dve.wait_ge(s_dh, n + 1)
                    nc.vector.tensor_tensor(wdl[u][:], wdr[u][:], f32(wdh[u][:]), ALU.subtract).then_inc(s_dl, 1)

                def first(b, nt):
                    dve.wait_ge(s_hh, b + 1)
                    w = nt * P
                    nc.vector.tensor_tensor(hl[:, :, :w], hr[:, :, :w], f32(hh[:, :, :w]), ALU.subtract).then_inc(s_hl, 1)

                def step(b, nt, j, u):
                    n = b * NJ + j
                    w = nt * P
                    more = not (isinstance(j, int) and j + 1 == NJ and isinstance(b, int) and b == NBL - 1)
                    if more:
                        split_gate(b, j + 1, 1 - u)
                    dve.wait_ge(s_pu, n + 1)
                    dve.wait_ge(s_sg, n + 1)
                    after(dve, s_al, n)
                    nc.vector.tensor_tensor(a[:, :w], sg[:, :w], pu[:, :w], ALU.mult).then_inc(s_a, 1)
                    dve.wait_ge(s_a, n + 1)
                    after(dve, s_dn, n - 1)
                    nc.vector.tensor_copy(ah[u][:, :w], a[:, :w]).then_inc(s_ah, 1)
                    dve.wait_ge(s_ah, n + 1)
                    nc.vector.tensor_tensor(al[u][:, :w], a[:, :w], f32(ah[u][:, :w]), ALU.subtract).then_inc(s_al, 1)
                    if more:
                        split_down(b, j + 1, 1 - u)

                def last(b, nt):
                    dve.wait_ge(s_dn, NJ * (b + 1))
                    after(dve, s_y2, 3 * b)
                    nc.vector.tensor_copy(ys[:, 1, 512:], py[:, 1, 512:])
                    if nt == 3:
                        nc.vector.tensor_copy(ys[:, 2, :], py[:, 2, :])
                    dve.drain().then_inc(s_yv, 1)
                    dve.wait_ge(s_ss, 3 * b + nt)
                    nc.vector.tensor_scalar(vv[:, :nt], ss[:, :nt], 1.0 / D, EPS, ALU.mult, ALU.add).then_inc(s_vv, 1)
                    dve.wait_ge(s_rr, b + 1)
                    for q in range(nt):
                        nc.vector.scalar_tensor_tensor(ys[:, q, :], ys[:, q, :], rr[:, q:q + 1], g_post[:], ALU.mult,
                                                       ALU.mult).then_inc(s_y1, 1)

                split_gate(0, 0, 0)
                split_down(0, 0, 0)
                walk(dve, first, step, last)


def encoder(nc, t):
    with ExitStack() as keep:
        neg_c = keep.enter_context(nc.sbuf_tensor("neg_c", [P, SEQ // P, H], F32))
        with ExitStack() as ctx:
            xhi = ctx.enter_context(nc.sbuf_tensor("xhi", [P, KD, TOK], F32R))
            xlo = ctx.enter_context(nc.sbuf_tensor("xlo", [P, KD, TOK], F32R))
            norm_inputs(nc, t, xhi, xlo)
            project_in(nc, t, xhi, xlo)
        forget(nc, t, neg_c)
        with ExitStack() as ctx:
            dhi = ctx.enter_context(nc.sbuf_tensor("dhi", [P, H, 2 * P], F32R))
            dlo = ctx.enter_context(nc.sbuf_tensor("dlo", [P, H, 2 * P], F32R))
            m_fox = ctx.enter_context(nc.sbuf_tensor("m_fox", [P, 2 * P], F32R))
            m_old = ctx.enter_context(nc.sbuf_tensor("m_old", [P, 2 * P], F32R))
            cols = ctx.enter_context(nc.sbuf_tensor("cols", [P, 2 * H, SEQ // P], F32))
            rel_tables(nc, t, dhi, dlo, m_fox, m_old, cols, neg_c)
            attend_prompt(nc, t, dhi, dlo, m_fox, m_old, cols)
    attend_streams(nc, t)
    mix_out(nc, t)
    feed_forward(nc, t)


_SCRATCH = {"fT": (H, TOK), "csum": (NB * H, PAST_A + NQ), "skew": (H, P, 3 * P), "skew2": (H, NQ, PAST_B + 2 * NQ),
            "mixT": (D, TOK), "x1": (TOK, D), "hT": (P, KD, TOK)}
_OUTPUTS = {"y": (TOK, D), "zT": (4 * GW, TOK), "v": (TOK, 2 * GW), "lfT": (H, TOK)}


def kernel(**inputs):
    import numpy as np
    import concourse.bacc as bacc
    from concourse.bass_utils import run_bass_kernel_spmd

    a = {k: np.asarray(v) for k, v in inputs.items()}
    lay = np.ascontiguousarray
    x = np.concatenate([a["x_prompt"].reshape(-1, D), a["x_sample"].reshape(-1, D)])
    w_in = a["w_in"][0]
    ka, kb = 3 * GW, 3 * GW + H
    w_qk = np.concatenate([w_in[:, 0:2 * GW], w_in[:, kb:kb + 2 * GW]], axis=1)
    w_v = np.concatenate([w_in[:, 2 * GW:3 * GW], w_in[:, kb + 2 * GW:kb + 3 * GW]], axis=1)

    def chunks(w, cols):
        return lay(w.reshape(-1, P, w.shape[1] // cols, cols).transpose(2, 1, 0, 3))

    def feature_column(g):
        return lay(g.reshape(KD, P).T)

    def keys_major(c):
        return lay(c.reshape(NB, -1, GW // P, P).transpose(0, 3, 2, 1))

    data = {
        "xT": lay(x.T.reshape(KD, P, TOK).transpose(1, 0, 2)),
        "x": lay(x),
        "g_pre": feature_column(a["norm_mix_pre"][0]),
        "w_slab": np.concatenate([chunks(w_qk, 256), chunks(w_v, 256)]),
        "w_f": chunks(w_in[:, ka:kb], H)[0],
        "b_forget": lay(a["b_forget"].reshape(H, 1)),
        "cache_logf": lay(a["cache_a_logf"][0].transpose(0, 2, 1).reshape(NB * H, PAST_A)),
        "rel_bias": lay(a["rel_bias"][0]),
        "cache_ak": keys_major(a["cache_a_k"][0]),
        "cache_bk": keys_major(a["cache_b_k"][0]),
        "cache_av": lay(a["cache_a_v"][0].reshape(NB, PAST_A, GW)),
        "cache_bv": lay(a["cache_b_v"][0].reshape(NB, PAST_B, GW)),
        "g_mix": feature_column(np.concatenate([a["gain_out_a"][0], a["gain_out_b"][0]])),
        "g_ffn": feature_column(a["norm_ffn_pre"][0]),
        "g_post": lay(a["norm_mix_post"]),
        "g_fpost": lay(a["norm_ffn_post"]),
        "w_out": lay(a["w_out"][0].reshape(KD, P, D)),
        "w_gu": lay(np.stack([chunks(a["w_gate"][0], P), chunks(a["w_up"][0], P)], axis=2)),
        "w_dn": lay(a["w_down"][0].reshape(NJ, P, D)),
    }

    nc = bacc.Bacc("TRN2", target_bir_lowering=False, num_devices=1)
    t = {k: nc.dram_tensor(f"in_{k}", v.shape, mybir.dt.from_np(v.dtype), kind="ExternalInput").ap() for k, v in data.items()}
    t |= {k: nc.dram_tensor(f"mid_{k}", s, F32, kind="Internal").ap() for k, s in _SCRATCH.items()}
    t |= {k: nc.dram_tensor(f"out_{k}", s, F32, kind="ExternalOutput").ap() for k, s in _OUTPUTS.items()}
    encoder(nc, t)
    r = run_bass_kernel_spmd(nc, [{f"in_{k}": v for k, v in data.items()}], core_ids=[0]).results[0]
    y, z, v, lf = (r[f"out_{k}"] for k in ("y", "zT", "v", "lfT"))

    def heads(m, streams):
        m = m[SEQ:].reshape(NB, NQ, H, HD) if streams else m[:SEQ].reshape(1, SEQ, H, HD)
        return lay(m[None])

    k_a, k_b, v_a, v_b = z[GW:2 * GW].T, z[3 * GW:4 * GW].T, v[:, :GW], v[:, GW:]
    keep = min(PAST_B, SEQ)
    return (lay(y[:SEQ].reshape(1, SEQ, D)), lay(y[SEQ:].reshape(NB, NQ, D)),
            heads(k_a, False), heads(v_a, False), lay(lf[:, :SEQ].T.reshape(1, 1, SEQ, H)),
            lay(heads(k_b, False)[:, :, SEQ - keep:]), lay(heads(v_b, False)[:, :, SEQ - keep:]),
            heads(k_a, True), heads(v_a, True), lay(lf[:, SEQ:].T.reshape(1, NB, NQ, H)),
            heads(k_b, True), heads(v_b, True))
```
